# Optimizing a Trainium2 kernel written in Bass

```python
import jax, jax.numpy as jnp
from jax import lax
import numpy as np

D_MODEL = 1024
BATCH = 1
SEQ = 256
DEPTH = 2

N_META = 16
N_HEADS = 16
N_KV_HEADS = 4
HEAD_DIM = 64
GQA_GROUP = N_HEADS // N_KV_HEADS
WINDOW = 128
BLOCK = 128
FRONT_PAD = (-N_META) % BLOCK
POOL_WINDOWS = (2, 4, 8, 16)
N_POOL_GROUPS = len(POOL_WINDOWS)
POOL_GROUP_DIM = D_MODEL // 8
POOL_DIM = N_POOL_GROUPS * POOL_GROUP_DIM
Q_DIM = N_HEADS * HEAD_DIM
KV_DIM = N_KV_HEADS * HEAD_DIM
IN_COLS = POOL_DIM + Q_DIM + 2 * KV_DIM + 2 * D_MODEL
SPLITS = [POOL_DIM, POOL_DIM + Q_DIM, POOL_DIM + Q_DIM + KV_DIM,
          POOL_DIM + Q_DIM + 2 * KV_DIM, POOL_DIM + Q_DIM + 2 * KV_DIM + D_MODEL]
D_FF = ((8 * D_MODEL // 3 + 127) // 128) * 128
RMS_EPS = 1e-6
NEG_INF = -1e30
FFN1_PRE, FFN1_POST, MIX_PRE, MIX_POST, FFN2_PRE, FFN2_POST = range(6)

kernel_name = "hybrid_pool_swa_gated_macaron"

def rmsnorm(x, g):
    xf = x.astype(jnp.float32)
    y = xf * lax.rsqrt(jnp.mean(xf * xf, axis=-1, keepdims=True) + RMS_EPS)
    return (y * g.astype(jnp.float32)).astype(x.dtype)

def swiglu(x, w_in, w_out):
    gate, up = jnp.split(x @ w_in, 2, axis=-1)
    return (jax.nn.silu(gate) * up) @ w_out

def alibi_slopes():
    m = 2.0 ** (-8.0 * np.arange(1, N_HEADS + 1) / N_HEADS)
    return jnp.asarray(m, dtype=jnp.float32).reshape(N_KV_HEADS, GQA_GROUP)

def pool_mixer(u, w_grp, scale, w_proj):
    B, L, _ = u.shape
    ug = u.reshape(B, L, N_POOL_GROUPS, POOL_GROUP_DIM)
    cs = jnp.cumsum(ug.astype(jnp.float32), axis=1)
    cs = jnp.pad(cs, ((0, 0), (1, 0), (0, 0), (0, 0)))
    t1 = jnp.arange(1, L + 1, dtype=jnp.int32)[:, None]
    win = jnp.asarray(POOL_WINDOWS, dtype=jnp.int32)[None, :]
    lag = jnp.maximum(t1 - win, 0)
    lagged = cs[:, lag, jnp.arange(N_POOL_GROUPS)[None, :], :]
    count = jnp.minimum(t1, win).astype(jnp.float32)
    pooled = (cs[:, 1:] - lagged) / count[None, :, :, None]
    mixed = (pooled - ug.astype(jnp.float32)).astype(u.dtype)
    mixed = jnp.einsum('blgc,gcd->blgd', mixed, w_grp).reshape(B, L, POOL_DIM) * scale
    return mixed @ w_proj

def swa_attention(q, k, v, sinks):
    B, L = q.shape[0], q.shape[1]
    Lp = L + FRONT_PAD
    nb = Lp // BLOCK
    padf = lambda a: jnp.pad(a, ((0, 0), (FRONT_PAD, 0), (0, 0), (0, 0)))
    qb = padf(q).reshape(B, nb, BLOCK, N_KV_HEADS, GQA_GROUP, HEAD_DIM)
    kb = padf(k).reshape(B, nb, BLOCK, N_KV_HEADS, HEAD_DIM)
    vb = padf(v).reshape(B, nb, BLOCK, N_KV_HEADS, HEAD_DIM)
    shift = lambda a: jnp.concatenate([jnp.zeros_like(a[:, :1]), a[:, :-1]], axis=1)
    kk = jnp.concatenate([shift(kb), kb], axis=2)
    vv = jnp.concatenate([shift(vb), vb], axis=2)
    k_meta, v_meta = k[:, :N_META], v[:, :N_META]
    scale = HEAD_DIM ** -0.5
    s_band = jnp.einsum('bnqkgd,bnskd->bnkgqs', qb, kk,
                        preferred_element_type=jnp.float32) * scale
    s_meta = jnp.einsum('bnqkgd,bmkd->bnkgqm', qb, k_meta,
                        preferred_element_type=jnp.float32) * scale
    q_pos = jnp.arange(Lp, dtype=jnp.int32).reshape(nb, BLOCK)
    k_pos = (jnp.arange(nb, dtype=jnp.int32)[:, None] - 1) * BLOCK + jnp.arange(2 * BLOCK, dtype=jnp.int32)[None, :]
    dist = q_pos[:, :, None] - k_pos[:, None, :]
    band_ok = (dist >= 0) & (dist < WINDOW) & (k_pos[:, None, :] >= FRONT_PAD)
    alibi_d = jnp.where(k_pos[:, None, :] >= FRONT_PAD + N_META, dist, 0).astype(jnp.float32)
    slopes = alibi_slopes()
    bias_band = jnp.where(band_ok[:, None, None],
                          -slopes[None, :, :, None, None] * alibi_d[:, None, None],
                          NEG_INF)
    s_band = s_band + bias_band[None]
    meta_pos = FRONT_PAD + jnp.arange(N_META, dtype=jnp.int32)
    meta_ok = (q_pos[:, :, None] - meta_pos[None, None, :]) >= WINDOW
    s_meta = jnp.where(meta_ok[None, :, None, None], s_meta, NEG_INF)
    sink = sinks.astype(jnp.float32).reshape(N_KV_HEADS, GQA_GROUP)[None, None, :, :, None, None]
    sink = jnp.broadcast_to(sink, s_band.shape[:-1] + (1,))
    logits = jnp.concatenate([s_band, s_meta, sink], axis=-1)
    probs = jax.nn.softmax(logits, axis=-1).astype(v.dtype)
    p_band = probs[..., :2 * BLOCK]
    p_meta = probs[..., 2 * BLOCK:2 * BLOCK + N_META]
    out = (jnp.einsum('bnkgqs,bnskd->bnqkgd', p_band, vv)
           + jnp.einsum('bnkgqm,bmkd->bnqkgd', p_meta, v_meta))
    return out.reshape(B, Lp, Q_DIM)[:, FRONT_PAD:]

def setup_inputs(seed: int = 0) -> dict:
    key = jax.random.key(seed)
    ks = jax.random.split(key, 13)
    nrm = lambda k, shape, fan_in: jax.random.normal(k, shape, jnp.float32) * (fan_in ** -0.5)
    x = jax.random.normal(ks[0], (BATCH, SEQ, D_MODEL), jnp.float32)
    meta_tokens = jax.random.normal(ks[1], (N_META, D_MODEL), jnp.float32)
    norm_g = 1.0 + 0.05 * jax.random.normal(ks[2], (DEPTH, 6, D_MODEL), jnp.float32)
    ffn_w_in = nrm(ks[3], (DEPTH, 2, D_MODEL, 2 * D_FF), D_MODEL)
    ffn_w_out = nrm(ks[4], (DEPTH, 2, D_FF, D_MODEL), D_FF)
    w_in = nrm(ks[5], (DEPTH, D_MODEL, IN_COLS), D_MODEL)
    pool_w_grp = nrm(ks[6], (DEPTH, N_POOL_GROUPS, POOL_GROUP_DIM, POOL_GROUP_DIM), POOL_GROUP_DIM)
    pool_scale = 1.0 + 0.05 * jax.random.normal(ks[7], (DEPTH, POOL_DIM), jnp.float32)
    w_pool_proj = nrm(ks[8], (DEPTH, POOL_DIM, D_MODEL), POOL_DIM)
    sinks = 0.5 * jax.random.normal(ks[9], (DEPTH, N_HEADS), jnp.float32)
    w_attn_proj = nrm(ks[10], (DEPTH, Q_DIM, D_MODEL), Q_DIM)
    w_o = nrm(ks[11], (DEPTH, D_MODEL, D_MODEL), D_MODEL)
    return {"x": x, "meta_tokens": meta_tokens, "norm_g": norm_g,
            "ffn_w_in": ffn_w_in, "ffn_w_out": ffn_w_out, "w_in": w_in,
            "pool_w_grp": pool_w_grp, "pool_scale": pool_scale,
            "w_pool_proj": w_pool_proj, "sinks": sinks,
            "w_attn_proj": w_attn_proj, "w_o": w_o}

def reference(x, meta_tokens, norm_g, ffn_w_in, ffn_w_out, w_in, pool_w_grp,
              pool_scale, w_pool_proj, sinks, w_attn_proj, w_o):
    B = x.shape[0]
    meta = jnp.broadcast_to(meta_tokens.astype(x.dtype)[None], (B, N_META, D_MODEL))
    h = jnp.concatenate([meta, x], axis=1)
    L = h.shape[1]
    for l in range(DEPTH):
        g = norm_g[l]
        h = h + 0.5 * rmsnorm(swiglu(rmsnorm(h, g[FFN1_PRE]), ffn_w_in[l, 0], ffn_w_out[l, 0]), g[FFN1_POST])
        hn = rmsnorm(h, g[MIX_PRE])
        u_pool, q, k, v, gate_pool, gate_attn = jnp.split(hn @ w_in[l], SPLITS, axis=-1)
        y_pool = pool_mixer(u_pool, pool_w_grp[l], pool_scale[l], w_pool_proj[l])
        attn = swa_attention(q.reshape(B, L, N_HEADS, HEAD_DIM),
                             k.reshape(B, L, N_KV_HEADS, HEAD_DIM),
                             v.reshape(B, L, N_KV_HEADS, HEAD_DIM), sinks[l])
        y_attn = attn @ w_attn_proj[l]
        merged = jax.nn.sigmoid(gate_pool) * y_pool + jax.nn.sigmoid(gate_attn) * y_attn
        h = h + rmsnorm(merged @ w_o[l], g[MIX_POST])
        h = h + 0.5 * rmsnorm(swiglu(rmsnorm(h, g[FFN2_PRE]), ffn_w_in[l, 1], ffn_w_out[l, 1]), g[FFN2_POST])
    return h[:, N_META:]


_drawn_inputs = setup_inputs


def setup_inputs(seed=0):
    import zlib

    import numpy as np

    out = dict(_drawn_inputs(seed))
    spreads = {}
    factors = {'sinks': 5.523}
    for name, (base, spread) in spreads.items():
        noise = np.random.default_rng([zlib.crc32(name.encode()), seed]).standard_normal(out[name].shape)
        drawn = base * np.exp(spread * noise) if base else spread * noise
        out[name] = __import__('jax').numpy.asarray(drawn.astype(out[name].dtype))
    for name, factor in factors.items():
        out[name] = (out[name] * factor).astype(out[name].dtype)
    return out
```

```python
from contextlib import ExitStack

import numpy as np
import concourse.bass as bass
from concourse import mybir

F32 = mybir.dt.float32
F32R = mybir.dt.float32r
ALU = mybir.AluOpType
ACT = mybir.ActivationFunctionType
AX_X = mybir.AxisListType.X
ds = bass.ds

P = 128
D = 1024
SEQ = 256
META = 16
T = META + SEQ
DEPTH = 2
HEADS, KV_HEADS, DH = 16, 4, 64
WINDOW = 128
POOL_WINDOWS = (2, 4, 8, 16)
GROUPS = len(POOL_WINDOWS)
POOL_DIM = GROUPS * P
Q_DIM = HEADS * DH
KV_DIM = KV_HEADS * DH
FF = ((8 * D // 3 + 127) // 128) * 128
EPS = 1e-6
KD = D // P
KF = FF // P
UW = 2 * P
RING = 4
OUT_K = (6, 5, 6, 5)
OUT_K0 = (0, 6, 11, 17)
B1, B2 = slice(META, META + P), slice(META + P, T)
BAND = T + META + P
FAR = 1e33
PAD = POOL_WINDOWS[-1]

U_FFN_IN = (0, 66)
U_FFN_OUT = (22, 88)
U_K, U_V, U_Q, U_POOL, U_GATE, U_PP, U_AP, U_WO = 38, 39, 40, 44, 46, 54, 58, 62
UNITS = 104
N_IN, N_OUT = FF * 2 // UW, 16
assert N_IN == 22 and sum(OUT_K) == KF and UNITS % RING == 0
T_FFN_IN, T_FFN_OUT = (0, 108), (44, 152)
T_KV, T_Q, T_POOL, T_GATE, T_PP, T_AP, T_WO = 52, 56, 64, 68, 84, 92, 100
TILES = 160
F_FFN_IN, F_FFN_OUT = (0, 54), (22, 76)
F_KV, F_Q, F_POOL, F_GATE, F_PP, F_AP, F_WO = 26, 28, 32, 34, 42, 46, 50
FINISHERS = 80
NORMS = 6


def slopes():
    return [2.0 ** (-8.0 * (h + 1) / HEADS) for h in range(HEADS)]


def head_at(i):
    tile, side = divmod(i, 2)
    group, t = divmod(tile, 4)
    return 8 * group + 4 * side + t


def kv_at(i):
    tile, side = divmod(i, 2)
    return 2 * (tile // 4) + side


def unit_k(u):
    for first in U_FFN_OUT:
        if first <= u < first + N_OUT:
            return OUT_K[(u - first) % 4]
    return GROUPS if U_PP <= u < U_AP else KD


def unit_dmas(u):
    return 2 if U_Q <= u < U_POOL else 4 if U_AP <= u < U_WO else 1


SLOT_DMAS = [sum(unit_dmas(u) for u in range(s, UNITS, RING)) for s in range(RING)]


def landed_at(u, layer, more=0):
    upto = sum(unit_dmas(v) for v in range(u % RING, u + 1, RING))
    return (layer * SLOT_DMAS[u % RING] + upto + more) * 16


def trunk(nc, x, meta_tokens, norm_g, ffn_w_in, ffn_w_out, w_in, pool_w_grp, pool_scale, w_pool_proj,
          sinks, w_attn_proj, w_o, geometry, out):
    with ExitStack() as ctx:
        def sb(name, shape, dt=F32):
            return ctx.enter_context(nc.sbuf_tensor(name, shape, dt))

        def sem(name):
            return ctx.enter_context(nc.semaphore(name))

        raw = sb("raw", [P, RING, KD * UW])
        w_hi = sb("w_hi", [P, RING, KD * UW], F32R)
        w_lo = sb("w_lo", [P, RING, KD * UW], F32R)
        h = sb("h", [P, KD, T])
        x_hi = sb("x_hi", [P, KD, T], F32R)
        x_lo = sb("x_lo", [P, KD, T], F32R)
        y = sb("y", [P, KD, T])
        sq = sb("sq", [P, 2, T])
        acc = sb("acc", [P, T])
        r = sb("r", [P, T])
        tmp = sb("tmp", [P, 2, PAD + T])
        var = sb("var", [P, 4])
        rt = sb("rt", [P, 4])
        half = sb("half", [P, 4])
        ident = sb("ident", [P, P])
        ones = sb("ones", [P, 1])
        g_all = sb("g_all", [P, DEPTH * NORMS * KD + DEPTH * GROUPS])
        g_cur = sb("g_cur", [P, NORMS * KD])
        scale_cur = sb("scale_cur", [P, GROUPS])
        sink_all = sb("sink_all", [P, DEPTH * HEADS])
        sink_cur = sb("sink_cur", [P, HEADS])
        geo = sb("geo", [P, BAND + HEADS * META + GROUPS * PAD])
        distance = geo[:, 0:BAND]
        causal0 = geo[0:META, BAND:BAND + HEADS * META].rearrange("p (h k) -> p h k", h=HEADS)
        ramp = geo[:, BAND + HEADS * META:].rearrange("p (g t) -> p g t", g=GROUPS)

        def shared_sizes(items):
            return sum(-(-int(np.prod(s[1:])) * 4 // 32) * 32 for _, s, _ in items)

        ffn_items = [("hid_hi", [P, KF, T], F32R), ("hid_lo", [P, KF, T], F32R), ("gate_r", [P, 2, T], F32),
                     ("silu", [P, 2, T], F32), ("up_r", [P, 2, T], F32), ("hid_f", [P, 2, T], F32)]
        mix_items = [("kT", [P, 2, T], F32), ("v_tok", [P, 2, KV_DIM], F32), ("v_meta", [META, KV_DIM], F32),
                     ("gates", [P, 2 * KD, T], F32), ("pool_u", [P, GROUPS, PAD + T], F32),
                     ("z_hi", [P, GROUPS, T], F32R),
                     ("z_lo", [P, GROUPS, T], F32R), ("o_hi", [P, KD, T], F32R), ("o_lo", [P, KD, T], F32R),
                     ("s", [P, 3, BAND], F32), ("pT", [P, 2, 3 * P], F32), ("pT_meta", [META, 2, 2 * P], F32),
                     ("s0", [32, HEADS, 32], F32), ("stats0", [META, 4, HEADS], F32),
                     ("stats", [P, 3, 8], F32), ("w_grp", [P, GROUPS, P], F32)]
        arena_bytes = max(shared_sizes(ffn_items), shared_sizes(mix_items))
        arena = sb("arena", [P, arena_bytes // 4])
        base = nc.sbuf_base - arena_bytes

        def place(items):
            at, placed = base, []
            for name, shape, dt in items:
                placed.append(nc.alloc_sbuf_tensor_at(name, shape, dt, offset=at))
                at += shared_sizes([(name, shape, dt)])
            return placed

        hid_hi, hid_lo, gate_r, silu, up_r, hid_f = place(ffn_items)
        (kT, v_tok, v_meta, gates, pool_u, z_hi, z_lo, o_hi, o_lo, s_buf, pT, pT_meta, s0, stats0,
         stats, w_grp) = place(mix_items)
        win = tmp
        p0T = sq[0:32].rearrange("p a t -> p (a t)")[:, 0:HEADS * 32].rearrange("p (h k) -> p h k", h=HEADS)
        qT = y
        vT = gates[:, 2 * KD - 2:2 * KD, :]
        first_x = gates[:, 0:8, :].rearrange("p a t -> p (a t)")[:, 0:2 * D].rearrange("p (b d) -> p b d", b=2)
        first_meta = gates[0:META, 8:12, :].rearrange("p a t -> p (a t)")[:, 0:D]
        n_rows = DEPTH * NORMS * KD + DEPTH * GROUPS
        first_rows = gates[0:n_rows, 12, 0:P]
        out_sb = gates[:, 0:8, :].rearrange("p a t -> p (a t)")[:, 0:2 * D].rearrange("p (b d) -> p b d", b=2)

        bank = [ctx.enter_context(nc.psum_tensor(f"bank{b}", [P, 512], F32)) for b in range(8)]
        score_bank = (bank[2], bank[3])
        pT_bank, pTm_bank, o_bank, small = bank[4], bank[5], bank[6], bank[7]
        S_SUM, S_BC = 0, 128

        inputs_in = sem("inputs_in")
        raw_landed = [sem(f"raw_landed{s}") for s in range(RING)]
        w_grp_in = sem("w_grp_in")
        out_stored = sem("out_stored")
        consts = sem("consts")
        hi_done = sem("hi_done")
        lo_done = sem("lo_done")
        unit_done = sem("unit_done")
        first_done = sem("first_done")
        tile_read = sem("tile_read")
        layer_consts = sem("layer_consts")
        first_T = sem("first_T")
        rows_read = sem("rows_read")
        h_ready = sem("h_ready")
        t_ready = sem("t_ready")
        xhi_ready = sem("xhi_ready")
        xlo_ready = sem("xlo_ready")
        sq_done = sem("sq_done")
        acc_done = sem("acc_done")
        ssq_done = sem("ssq_done")
        var_ready = sem("var_ready")
        rt_ready = sem("rt_ready")
        bcast_done = sem("bcast_done")
        r_ready = sem("r_ready")
        silu_done = sem("silu_done")
        hf_ready = sem("hf_ready")
        hid_hi_ready = sem("hid_hi_ready")
        hid_ready = sem("hid_ready")
        v_turned = sem("v_turned")
        v_ready = sem("v_ready")
        s0_done = sem("s0_done")
        s0_step = sem("s0_step")
        s0_exp = sem("s0_exp")
        score_done = sem("score_done")
        biased = sem("biased")
        row_max = sem("row_max")
        neg_max = sem("neg_max")
        exp_done = sem("exp_done")
        den_ready = sem("den_ready")
        inv_ready = sem("inv_ready")
        p_ready = sem("p_ready")
        pT_done = sem("pT_done")
        pT_ready = sem("pT_ready")
        o_done = sem("o_done")
        ohi_ready = sem("ohi_ready")
        olo_ready = sem("olo_ready")
        tanh_done = sem("tanh_done")
        win_step = sem("win_step")
        win_done = sem("win_done")
        mixed_ready = sem("mixed_ready")
        grp_done = sem("grp_done")
        zhi_ready = sem("zhi_ready")
        zlo_ready = sem("zlo_ready")
        merged = sem("merged")
        final_T = sem("final_T")
        out_ready = sem("out_ready")

        def split_parts(u):
            s, n = u % RING, unit_k(u) * UW
            if not U_Q <= u < U_POOL:
                return [(raw[:, s, 0:n], w_hi[:, s, 0:n], w_lo[:, s, 0:n])]
            from_raw = raw[:, s, :].rearrange("p (k s t c) -> p t k s c", s=2, t=2, c=DH)
            to_hi, to_lo = (w[:, s, :].rearrange("p (k t s c) -> p t k s c", s=2, t=2, c=DH) for w in (w_hi, w_lo))
            return [(from_raw[:, t], to_hi[:, t], to_lo[:, t]) for t in range(2)]

        block = ctx.enter_context(nc.Block())

        WIN_STEPS = sum(g + 2 for g in range(GROUPS))

        @block.sync
        def _(sp):
            sp.dma_start(first_x, x[0].rearrange("(b p) d -> p b d", b=2)).then_inc(inputs_in, 16)
            sp.dma_start(first_meta, meta_tokens).then_inc(inputs_in, 16)
            sp.dma_start(first_rows[0:DEPTH * NORMS * KD, :], norm_g.rearrange("l n (k p) -> (l n k) p", p=P)
                         ).then_inc(inputs_in, 16)
            sp.dma_start(first_rows[DEPTH * NORMS * KD:n_rows, :], pool_scale.rearrange("l (g p) -> (l g) p", p=P)
                         ).then_inc(inputs_in, 16)
            sp.dma_start(geo[:, :], geometry).then_inc(inputs_in, 16)
            sp.dma_start(sink_all[:, :], sinks.rearrange("(o l) h -> o (l h)", o=1).to_broadcast([P, DEPTH * HEADS])
                         ).then_inc(inputs_in, 16)

            def slot_free(u, l, more=0):
                sp.wait_ge(lo_done, l * UNITS + u + 1 + more)

            def load(u, src, dst=None):
                s = u % RING
                to = raw[:, s, 0:unit_k(u) * UW].rearrange("p (k c) -> p k c", c=UW) if dst is None else dst
                sp.dma_start(to, src).then_inc(raw_landed[s], 16)

            def ffn_loads(l, f):
                w1 = ffn_w_in[ds(l, 1), f].rearrange("o (k p) n -> p (o k) n", p=P)
                w2 = ffn_w_out[ds(l, 1), f].rearrange("o (k p) n -> p (o k) n", p=P)
                u0 = U_FFN_IN[f]
                for j in range(2):
                    slot_free(u0 + j, l)
                    load(u0 + j, w1[:, :, j * FF:j * FF + UW])
                with sp.Fori(0, N_IN - 5, 4) as i:
                    for j in range(4):
                        slot_free(u0 + 2 + j, l, i)
                        load(u0 + 2 + j, w1[:, :, ds(i * (UW // 2) + (UW * (1 + j // 2) + j % 2 * FF), UW)])
                u0 = U_FFN_OUT[f]
                with sp.Fori(0, N_OUT - 3, 4) as i:
                    for j in range(4):
                        slot_free(u0 + j, l, i)
                        load(u0 + j, w2[:, OUT_K0[j]:OUT_K0[j] + OUT_K[j], ds(i * (UW // 4), UW)])

            with sp.Fori(0, DEPTH) as l:
                ffn_loads(l, 0)
                w = w_in[ds(l, 1)].rearrange("o (k p) n -> p (o k) n", p=P)
                q0, k0 = POOL_DIM, POOL_DIM + Q_DIM
                v0, g0 = k0 + KV_DIM, k0 + 2 * KV_DIM
                for u in range(U_K, U_PP):
                    slot_free(u, l)
                    if u == U_POOL:
                        sp.wait_ge(unit_done, l * UNITS + U_K + RING)
                        sp.dma_start(w_grp[:, :, :], pool_w_grp[ds(l, 1)].rearrange("o g c d -> c (o g) d")
                                     ).then_inc(w_grp_in, 16)
                    if U_Q <= u < U_POOL:
                        c = q0 + (8 * ((u - U_Q) // 2) + 2 * ((u - U_Q) % 2)) * DH
                        to = raw[:, u % RING, :].rearrange("p (k s c) -> p k s c", s=2, c=P)
                        for side in range(2):
                            load(u, w[:, :, c + side * 4 * DH:c + side * 4 * DH + P], to[:, :, side, :])
                    else:
                        c = (k0 if u == U_K else v0 if u == U_V else (u - U_POOL) * UW if u < U_GATE
                             else g0 + (u - U_GATE) * UW)
                        load(u, w[:, :, c:c + UW])
                wp = w_pool_proj[ds(l, 1)].rearrange("o (k p) n -> p (o k) n", p=P)
                for m in range(4):
                    slot_free(U_PP + m, l)
                    load(U_PP + m, wp[:, :, m * UW:(m + 1) * UW])
                wa = w_attn_proj[ds(l, 1)].rearrange("o (g s t f) n -> g s f (o t) n", g=2, s=2, t=4)
                for m in range(4):
                    u = U_AP + m
                    slot_free(u, l)
                    to = raw[:, u % RING, :].rearrange("p (g t c) -> p g t c", g=2, t=4)
                    for g in range(2):
                        for side in range(2):
                            load(u, wa[g, side, :, :, m * UW:(m + 1) * UW], to[side * DH:(side + 1) * DH, g])
                wo = w_o[ds(l, 1)].rearrange("o (k p) n -> p (o k) n", p=P)
                for m in range(4):
                    slot_free(U_WO + m, l)
                    load(U_WO + m, wo[:, :, m * UW:(m + 1) * UW])
                ffn_loads(l, 1)

            for b in range(2):
                sp.wait_ge(out_ready, 2 * b + 2)
                sp.dma_start(out[0, b * P:(b + 1) * P, :], out_sb[:, b, :]).then_inc(out_stored, 16)
            sp.wait_ge(out_stored, 32)

        @block.tensor
        def _(pe):
            pe.sem_inc(unit_done, RING)
            pe.sem_inc(ssq_done, 1)

            def weights(u, k, mt):
                s = u % RING
                return [w[:, s, k * UW + mt * P:k * UW + (mt + 1) * P] for w in (w_hi, w_lo)]

            def products(ps, w, a_hi, a_lo, start, stop):
                pe.matmul(ps[:, 0:T], w[0], a_hi, start=start, stop=False)
                pe.matmul(ps[:, 0:T], w[0], a_lo, start=False, stop=False)
                return pe.matmul(ps[:, 0:T], w[1], a_hi, start=False, stop=stop)

            def unit_split(u, l, more=0):
                pe.wait_ge(lo_done, l * UNITS + u + RING + 1 + more)

            def tile_free(t, l, lag, more=0):
                pe.wait_ge(tile_read, l * TILES + t - lag + 1 + more)

            def deep_pair(u, l, a_hi, a_lo, operand_ready, extra=None, t=None):
                unit_split(u, l)
                unit_split(u + 1, l)
                for k in range(KD):
                    operand_ready(k)
                    for c in range(4):
                        if k == 0 and t is not None:
                            tile_free(t + c, l, 4)
                        if k == KD - 1 and c == 2 and extra is not None:
                            extra()
                        last = products(bank[c], weights(u + c // 2, k, c % 2), a_hi[:, k, :], a_lo[:, k, :],
                                        k == 0, k == KD - 1)
                        if k == KD - 1:
                            last.then_inc(first_done if c % 2 == 0 else unit_done, 1)

            def unit_tile(u, l, mt, b, nk, a_hi, a_lo):
                for k in range(nk):
                    last = products(bank[b], weights(u, k, mt), a_hi[:, k, :], a_lo[:, k, :], k == 0, k == nk - 1)
                last.then_inc(first_done if mt == 0 else unit_done, 1)

            def unit(u, l, t, banks, lag, nk, a_hi, a_lo, more=0, more_t=0):
                unit_split(u, l, more)
                for mt in range(2):
                    tile_free(t + mt, l, lag, more_t)
                    unit_tile(u, l, mt, banks[mt], nk, a_hi, a_lo)

            def sum_squares(q, l):
                pe.wait_ge(acc_done, (l * NORMS + q + 1) * (KD - 2))
                pe.wait_ge(sq_done, (l * NORMS + q + 1) * KD)
                pe.wait_ge(r_ready, l * NORMS + q + 1)
                for b in range(3):
                    n = min(P, T - b * P)
                    o = small[0:n, S_SUM + b:S_SUM + b + 1]
                    pe.matmul(o, acc[:, b * P:b * P + n], ones[:, 0:1], start=True, stop=False)
                    last = pe.matmul(o, sq[:, 1, b * P:b * P + n], ones[:, 0:1], start=False, stop=True)
                last.then_inc(ssq_done, 1)

            def spread_rms(q, l):
                pe.wait_ge(rt_ready, l * NORMS + q + 1)
                for b in range(3):
                    n = min(P, T - b * P)
                    last = pe.matmul(small[:, S_BC + b * P:S_BC + b * P + n], rt[0:n, b:b + 1].to_broadcast([n, P]),
                                     ident[0:n, 0:n], start=True, stop=True)
                last.then_inc(bcast_done, 1)

            def x_tile(n, l):
                pe.wait_ge(xlo_ready, l * 4 * KD + n + 1)

            def ffn(f, l):
                u0, t0 = U_FFN_IN[f], T_FFN_IN[f]
                deep_pair(u0, l, x_hi, x_lo, lambda k: x_tile((0, 3 * KD)[f] + k, l), lambda: sum_squares(4 * f, l))
                spread_rms(4 * f, l)
                with pe.Fori(0, (N_IN - 2) // 4) as i:
                    for j in range(4):
                        b = 2 * (j % 2)
                        unit(u0 + 2 + j, l, t0 + 4 + 2 * j, (b, b + 1), 4, KD, x_hi, x_lo, i * 4, i * 8)
                u0, t0 = U_FFN_OUT[f], T_FFN_OUT[f]
                with pe.Fori(0, N_OUT // 4) as i:
                    for j in range(4):
                        unit_split(u0 + j, l, i * 4)
                        pe.wait_ge(hid_ready, l * 2 * KF + f * KF + OUT_K0[j] + OUT_K[j])
                        for mt in range(2):
                            if j == 0:
                                tile_free(t0 + mt, l, 2, i * 2)
                            for k in range(OUT_K[j]):
                                kk = OUT_K0[j] + k
                                last = products(bank[mt], weights(u0 + j, k, mt), hid_hi[:, kk, :], hid_lo[:, kk, :],
                                                kk == 0, kk == KF - 1)
                            if mt == 0 and j == 3:
                                last.then_inc(first_done, 1)
                        last.then_inc(unit_done, 1)
                sum_squares(4 * f + 1, l)
                spread_rms(4 * f + 1, l)

            def turn_v():
                for j in range(2):
                    for b, blk in enumerate((B1, B2)):
                        pe.transpose(pT_bank[:, b * KV_DIM + j * P:b * KV_DIM + (j + 1) * P], vT[:, j, blk], ident[:, :])
                for j in range(2):
                    last = pe.transpose(pTm_bank[:, j * P:(j + 1) * P], vT[:, j, 0:P], ident[:, :])
                last.then_inc(v_turned, 1)

            def rows(i):
                return slice((i % 2) * DH, (i % 2) * DH + DH)

            def scores0(l):
                for i in range(HEADS):
                    last = pe.matmul((o_bank, small)[i % 2][0:META, i // 2 * META:(i // 2 + 1) * META], qT[rows(i), i // 2, 0:META],
                                     kT[rows(i), i // 8, 0:META], start=True, stop=True)
                last.then_inc(s0_done, 1)

            def scores(i, l):
                if i >= 2:
                    pe.wait_ge(biased, l * HEADS + i - 1)
                sc = score_bank[i % 2]
                pe.matmul(sc[:, 0:T], qT[rows(i), i // 2, B2], kT[rows(i), i // 8, 0:T], start=True, stop=True)
                pe.matmul(sc[:, T:BAND], qT[rows(i), i // 2, B1], kT[rows(i), i // 8, 0:META + P], start=True,
                          stop=True).then_inc(score_done, 1)

            def turn_p(i, l):
                pe.wait_ge(p_ready, l * HEADS + i + 1)
                if i >= 1:
                    pe.wait_ge(pT_ready, l * HEADS + i)
                s = s_buf[:, i % 3, :]
                pe.transpose(pT_bank[:, 0:P], s[:, T + META:BAND], ident[:, :])
                pe.transpose(pT_bank[:, P:2 * P], s[:, META:META + P], ident[:, :])
                pe.transpose(pT_bank[:, 2 * P:3 * P], s[:, META + P:T], ident[:, :])
                pe.transpose(pTm_bank[:, 0:P], s[:, T:T + P], ident[:, :])
                pe.transpose(pTm_bank[:, P:2 * P], s[:, 0:P], ident[:, :]).then_inc(pT_done, 1)

            def attend(i, l):
                pe.wait_ge(pT_ready, l * HEADS + i + 1)
                if i == 0:
                    pe.wait_ge(v_ready, 2 * l + 2)
                    pe.wait_ge(s0_step, (l + 1) * S0_STEPS)
                if i % 2 == 0 and i >= 2:
                    pe.wait_ge(olo_ready, l * KD + i // 2)
                o = o_bank[rows(i), :]
                c = slice(kv_at(i) * DH, (kv_at(i) + 1) * DH)
                pe.matmul(o[:, 0:META], v_meta[0:META, c], p0T[0:META, i, 0:META], start=True, stop=False,
                          skip_group_check=True)
                pe.matmul(o[:, META:T], v_meta[0:META, c], pT_meta[0:META, i % 2, :], start=False, stop=False,
                          skip_group_check=True)
                pe.matmul(o[:, META:T], v_tok[:, 0, c], pT[:, i % 2, 0:2 * P], start=False, stop=False,
                          skip_group_check=True)
                pe.matmul(o[:, META + P:T], v_tok[:, 1, c], pT[:, i % 2, 2 * P:3 * P], start=False, stop=True,
                          skip_group_check=True).then_inc(o_done, 1)

            def group(g, l):
                pe.wait_ge(mixed_ready, l * GROUPS + g + 1)
                if g == 0:
                    pe.wait_ge(w_grp_in, l * 16 + 16)
                    pe.wait_ge(r_ready, l * NORMS + 4)
                else:
                    pe.wait_ge(zlo_ready, l * GROUPS + g)
                pe.matmul(small[:, S_BC:S_BC + T], w_grp[:, g, :], pool_u[:, g, PAD:], start=True, stop=True
                          ).then_inc(grp_done, 1)

            pe.wait_ge(inputs_in, 16 * 6)
            pe.wait_ge(consts, 1)
            pe.transpose(small[:, 0:n_rows], first_rows, ident[0:n_rows, 0:n_rows]).then_inc(first_T, 1)
            for k in range(KD):
                if k >= 4:
                    pe.wait_ge(h_ready, k - 3)
                b = bank[k % 4]
                pe.transpose(b[:, 0:META], first_meta[:, k * P:(k + 1) * P], ident[0:META, 0:META])
                pe.transpose(b[:, B1], first_x[:, 0, k * P:(k + 1) * P], ident[:, :])
                pe.transpose(b[:, B2], first_x[:, 1, k * P:(k + 1) * P], ident[:, :]).then_inc(first_T, 1)

            with pe.Fori(0, DEPTH) as l:
                ffn(0, l)
                deep_pair(U_K, l, x_hi, x_lo, lambda k: x_tile(KD + k, l), lambda: sum_squares(2, l))
                spread_rms(2, l)
                for n in range(4):
                    b = 2 * (n % 2)
                    unit(U_Q + n, l, T_Q + 2 * n, (b, b + 1), 4, KD, x_hi, x_lo)
                    if n == 1:
                        turn_v()
                unit(U_POOL, l, T_POOL, (0, 1), 2, KD, x_hi, x_lo)
                scores0(l)
                unit(U_POOL + 1, l, T_POOL + 2, (2, 3), 4, KD, x_hi, x_lo)
                for i in range(HEADS + 3):
                    if i < HEADS:
                        u, mt = U_GATE + i // 2, i % 2
                        if mt == 0:
                            unit_split(u, l)
                        tile_free(T_GATE + i, l, 2)
                        unit_tile(u, l, mt, mt, KD, x_hi, x_lo)
                        if i == 0:
                            pe.wait_ge(tile_read, l * TILES + T_GATE)
                        scores(i, l)
                    if 2 <= i < HEADS + 2:
                        turn_p(i - 2, l)
                    if i >= 3:
                        attend(i - 3, l)
                    if i in GROUP_STEPS:
                        group(GROUP_STEPS.index(i), l)
                    if i >= HEADS:
                        m = i - HEADS
                        if m == 0:
                            pe.wait_ge(zlo_ready, (l + 1) * GROUPS)
                            pe.wait_ge(biased, (l + 1) * HEADS)
                        unit(U_PP + m, l, T_PP + 2 * m, (2 * (m % 2), 2 * (m % 2) + 1), 2 if m == 0 else 4,
                             GROUPS, z_hi, z_lo)
                unit(U_PP + 3, l, T_PP + 6, (2, 3), 4, GROUPS, z_hi, z_lo)
                pe.wait_ge(olo_ready, (l + 1) * KD)
                for m in range(4):
                    b = 2 * (m % 2)
                    unit(U_AP + m, l, T_AP + 2 * m, (b, b + 1), 4, KD, o_hi, o_lo)
                deep_pair(U_WO, l, x_hi, x_lo, lambda k: x_tile(2 * KD + k, l), t=T_WO)
                for m in range(2, 4):
                    b = 2 * (m % 2)
                    unit(U_WO + m, l, T_WO + 2 * m, (b, b + 1), 4, KD, x_hi, x_lo)
                sum_squares(3, l)
                spread_rms(3, l)
                ffn(1, l)

            pe.wait_ge(h_ready, KD * (3 * DEPTH + 1))
            for b in range(2):
                for half_d in range(2):
                    for k in range(4):
                        last = pe.transpose(bank[2 * b + half_d][:, k * P:(k + 1) * P],
                                            h[:, 4 * half_d + k, (B1, B2)[b]], ident[:, :])
                    last.then_inc(final_T, 1)

        @block.scalar
        def _(act):
            act.sem_inc(silu_done, 2)

            def split_hi(u, l, more=0):
                act.wait_ge(raw_landed[u % RING], landed_at(u, l, more))
                act.wait_ge(unit_done, l * UNITS + u + 1 + (more * 4))
                for w, hi, _ in split_parts(u):
                    last = act.activation(hi, w, ACT.Copy)
                last.then_inc(hi_done, 1)

            def square(q, l, m, src, ready, at):
                act.wait_ge(ready, at)
                if m < 2:
                    act.wait_ge(ssq_done, l * NORMS + q + 1)
                else:
                    act.wait_ge(acc_done, (l * NORMS + q) * (KD - 2) + max(1, m - 2))
                act.activation(sq[:, m % 2, :], src, ACT.Square).then_inc(sq_done, 1)

            def pre_norm(n, l):
                if n == 0:
                    act.wait_ge(layer_consts, l + 1)
                for k in range(KD):
                    act.wait_ge(h_ready, l * 3 * KD + n * KD + k + 1)
                    act.activation(x_hi[:, k, :], h[:, k, :], ACT.Copy,
                                   scale=g_cur[:, 2 * n * KD + k:2 * n * KD + k + 1]).then_inc(xhi_ready, 1)
                    square(2 * n, l, k, h[:, k, :], h_ready, l * 3 * KD + n * KD + k + 1)

            def silus(f, l, pair, more=0):
                for j in range(2):
                    act.wait_ge(tile_read, l * TILES + T_FFN_IN[f] + 4 * pair + j + 1 + more * 4)
                    act.wait_ge(hf_ready, l * 2 * KF + f * KF + 2 * pair + j + 1 + more * 2)
                    act.activation(silu[:, j, :], gate_r[:, j, :], ACT.Silu).then_inc(silu_done, 1)

            def ffn(f, l):
                u0 = U_FFN_IN[f]
                split_hi(u0 + 3, l)
                silus(f, l, 0)
                split_hi(u0 + 4, l)
                with act.Fori(0, 4) as i:
                    for j in range(4):
                        split_hi(u0 + 5 + j, l, i)
                        if j % 2 == 1:
                            silus(f, l, 1 + j // 2, i * 2)
                for j in range(18, 22):
                    split_hi(u0 + j + 3, l)
                    if j % 2 == 1:
                        silus(f, l, (j - 1) // 2)
                u0 = U_FFN_OUT[f]
                for i in range(4):
                    for j in range(4):
                        if u0 + 3 + 4 * i + j < UNITS:
                            split_hi(u0 + 3 + 4 * i + j, l)
                    for m in (2 * i, 2 * i + 1):
                        square(4 * f + 1, l, m, y[:, m, :], tile_read, l * TILES + T_FFN_OUT[f] + m + 1)

            def exps(i, l):
                act.wait_ge(neg_max, l * HEADS + i + 1)
                s, st = s_buf[:, i % 3, :], stats[:, i % 3, :]
                act.activation(s[:, 0:T], s[:, 0:T], ACT.Exp, bias=st[:, 2:3], accum_out=st[:, 4:5])
                act.activation(s[:, T:BAND], s[:, T:BAND], ACT.Exp, bias=st[:, 3:4], accum_out=st[:, 5:6])
                act.activation(st[:, 6:8], st[:, 2:4], ACT.Exp, bias=sink_cur[:, i:i + 1]).then_inc(exp_done, 1)

            def take_pT(i, l):
                act.wait_ge(pT_done, l * HEADS + i + 1)
                if i >= 2:
                    act.wait_ge(o_done, l * HEADS + i - 1)
                act.activation(pT[:, i % 2, :], pT_bank[:, 0:3 * P], ACT.Copy)
                act.activation(pT_meta[0:META, i % 2, :], pTm_bank[0:META, 0:2 * P], ACT.Copy).then_inc(pT_ready, 1)

            def tanh(m, l):
                act.wait_ge(tile_read, l * TILES + T_GATE + m + 1)
                act.activation(gates[:, m, :], gates[:, m, :], ACT.Tanh, scale=0.5).then_inc(tanh_done, 1)

            def merge_hi(m, l):
                act.wait_ge(merged, l * KD + m + 1)
                act.activation(x_hi[:, m, :], gates[:, m, :], ACT.Copy, scale=0.5).then_inc(xhi_ready, 1)

            with act.Fori(0, DEPTH) as l:
                for u in range(3):
                    split_hi(u, l)
                pre_norm(0, l)
                ffn(0, l)
                pre_norm(1, l)
                act.preload_act_table(ACT.Exp)
                for u in range(41, 45):
                    split_hi(u, l)
                act.wait_ge(v_turned, l + 1)
                act.activation(v_tok[:, :, :], pT_bank[:, :].rearrange("p (b c) -> p b c", b=2), ACT.Copy
                               ).then_inc(v_ready, 1)
                act.activation(v_meta[:, :], pTm_bank[0:META, 0:KV_DIM], ACT.Copy).then_inc(v_ready, 1)
                for u in range(45, 49):
                    split_hi(u, l)
                for i in range(HEADS + 3):
                    if i == 0:
                        act.wait_ge(s0_step, l * S0_STEPS + S0_SHIFTED)
                        act.activation(s0[0:META, :, 0:META], s0[0:META, :, 0:META], ACT.Exp)
                        act.activation(stats0[:, 2, :], stats0[:, 1, :], ACT.Exp).then_inc(s0_exp, 1)
                    if 1 <= i <= HEADS:
                        tanh(i - 1, l)
                    if i < HEADS:
                        exps(i, l)
                    if i % 2 == 0 and i < HEADS:
                        split_hi(49 + i // 2, l)
                    if i >= HEADS:
                        split_hi(57 + i - HEADS, l)
                    if 2 <= i < HEADS + 2:
                        take_pT(i - 2, l)
                split_hi(60, l)
                for n in range(4):
                    split_hi(61 + n, l)
                    if n >= 1:
                        merge_hi(2 * n - 2, l)
                        merge_hi(2 * n - 1, l)
                merge_hi(6, l)
                merge_hi(7, l)
                act.preload_act_table(ACT.Silu)
                split_hi(65, l)
                split_hi(66, l)
                for m in range(4):
                    square(3, l, m, y[:, m, :], tile_read, l * TILES + T_WO + m + 1)
                split_hi(67, l)
                for m in range(4, 6):
                    square(3, l, m, y[:, m, :], tile_read, l * TILES + T_WO + m + 1)
                split_hi(68, l)
                for m in range(6, 8):
                    square(3, l, m, y[:, m, :], tile_read, l * TILES + T_WO + m + 1)
                pre_norm(2, l)
                ffn(1, l)

        @block.vector
        def _(dve):
            dve.sem_inc(lo_done, RING)
            dve.sem_inc(r_ready, 1)

            def split_lo(u, l, more=0):
                dve.wait_ge(hi_done, l * UNITS + u + 1 + more)
                for w, hi, lo in split_parts(u):
                    last = dve.tensor_tensor(lo, w, hi.bitcast(F32), ALU.subtract)
                last.then_inc(lo_done, 1)

            def tile_done(u, fin, l, mt, more_u=0, more_f=0):
                if mt == 0:
                    dve.wait_ge(first_done, l * FINISHERS + fin + 1 + more_f)
                else:
                    dve.wait_ge(unit_done, l * UNITS + u + RING + 1 + more_u)

            def layer_columns(l):
                if_first = DEPTH * NORMS * KD
                dve.tensor_copy(g_cur[:, :], g_all[:, ds(l * (NORMS * KD), NORMS * KD)])
                dve.tensor_copy(scale_cur[:, :], g_all[:, ds(l * GROUPS + if_first, GROUPS)])
                for g in range(2):
                    last = dve.tensor_copy(sink_cur[:, 8 * g:8 * g + 8].rearrange("p (t s) -> p s t", s=2),
                                           sink_all[:, ds(l * HEADS + 8 * g, 8)].rearrange("p (s t) -> p s t", s=2))
                last.then_inc(layer_consts, 1)
                dve.wait_ge(layer_consts, l + 1)

            def mean_square(q, l):
                dve.wait_ge(ssq_done, l * NORMS + q + 2)
                dve.tensor_scalar(var[:, 0:2], small[:, S_SUM:S_SUM + 2], 1.0 / D, EPS, ALU.mult, ALU.add)
                n = T - 2 * P
                dve.tensor_scalar(var[0:n, 2:3], small[0:n, S_SUM + 2:S_SUM + 3], 1.0 / D, EPS, ALU.mult, ALU.add
                                  ).then_inc(var_ready, 1)

            def take_rms(q, l):
                dve.wait_ge(bcast_done, l * NORMS + q + 1)
                dve.tensor_copy(r[:, :], small[:, S_BC:S_BC + T]).then_inc(r_ready, 1)

            def rms_in(q, l):
                dve.wait_ge(r_ready, l * NORMS + q + 2)

            def add_update(n, l, k):
                j = l * 3 * KD + n * KD + k
                c = (2 * n + 1) * KD + k
                dve.scalar_tensor_tensor(out=tmp[:, k % 2, 0:T], in0=y[:, k, :], scalar=g_cur[:, c:c + 1], in1=r[:, :],
                                         op0=ALU.mult, op1=ALU.mult).then_inc(t_ready, 1)
                dve.wait_ge(t_ready, j + 1)
                dve.scalar_tensor_tensor(out=h[:, k, :], in0=tmp[:, k % 2, 0:T], scalar=1.0 if n == 1 else 0.5,
                                         in1=h[:, k, :], op0=ALU.mult, op1=ALU.add).then_inc(h_ready, 1)

            def x_low(n, l, k):
                at = (0, KD, 3 * KD)[n]
                dve.wait_ge(xhi_ready, l * 4 * KD + at + k + 1)
                dve.scalar_tensor_tensor(out=x_lo[:, k, :], in0=h[:, k, :],
                                         scalar=g_cur[:, 2 * n * KD + k:2 * n * KD + k + 1],
                                         in1=x_hi[:, k, :].bitcast(F32), op0=ALU.mult, op1=ALU.subtract
                                         ).then_inc(xlo_ready, 1)

            def boundary(n, l):
                q = 2 * n + 1
                mean_square(q, l)
                take_rms(q, l)
                rms_in(q, l)
                for k in range(KD):
                    add_update(n, l, k)
                    if n < 2 and k >= 1:
                        x_low(n + 1, l, k - 1)
                if n < 2:
                    x_low(n + 1, l, KD - 1)

            def take_gate(f, l, unit, mp=0):
                for j in range(2):
                    tile_done(U_FFN_IN[f] + unit, F_FFN_IN[f] + unit, l, j, mp * 2, mp * 2)
                    dve.wait_ge(silu_done, l * 2 * KF + f * KF + unit + j + 1 + mp * 2)
                    dve.tensor_tensor(gate_r[:, j, :], bank[j][:, 0:T], r[:, :], ALU.mult).then_inc(tile_read, 1)

            def take_up(f, l, unit, mp=0):
                for j in range(2):
                    tile_done(U_FFN_IN[f] + unit, F_FFN_IN[f] + unit, l, j, mp * 2, mp * 2)
                    dve.wait_ge(hf_ready, l * 2 * KF + f * KF + unit - 1 + j + 1 + mp * 2)
                    dve.tensor_tensor(up_r[:, j, :], bank[2 + j][:, 0:T], r[:, :], ALU.mult).then_inc(tile_read, 1)

            def ffn(f, l):
                u0 = U_FFN_IN[f]
                split_lo(u0 + 3, l)
                mean_square(4 * f, l)
                take_rms(4 * f, l)
                rms_in(4 * f, l)
                take_gate(f, l, 0)
                split_lo(u0 + 4, l)
                with dve.Fori(0, 4) as i:
                    for j in range(4):
                        split_lo(u0 + 5 + j, l, i * 4)
                        (take_up if j % 2 == 0 else take_gate)(f, l, 1 + j, i * 2)
                for j in range(18, 22):
                    split_lo(u0 + j + 3, l)
                    (take_up if j % 2 == 0 else take_gate)(f, l, j - 1, 0)
                take_up(f, l, 21, 0)
                u0 = U_FFN_OUT[f]
                for i in range(4):
                    for j in range(4):
                        if u0 + 3 + 4 * i + j < UNITS:
                            split_lo(u0 + 3 + 4 * i + j, l)
                    for j in range(2):
                        tile_done(u0 + 4 * i + 3, F_FFN_OUT[f] + i, l, j)
                        dve.tensor_copy(y[:, 2 * i + j, :], bank[j][:, 0:T]).then_inc(tile_read, 1)

            def take(u, fin, l, banks, how):
                for j in range(2):
                    tile_done(u, fin, l, j)
                    how(j, bank[banks[j]][:, 0:T]).then_inc(tile_read, 1)

            def take_q(n, l):
                b = 2 * (n % 2)
                take(U_Q + n, F_Q + n, l, (b, b + 1), lambda j, ps: dve.scalar_tensor_tensor(
                    out=qT[:, 2 * n + j, :], in0=ps, scalar=DH ** -0.5, in1=r[:, :], op0=ALU.mult, op1=ALU.mult))

            def take_pool(n, l):
                take(U_POOL + n, F_POOL + n, l, (2 * n, 2 * n + 1), lambda j, ps: dve.tensor_tensor(
                    pool_u[:, 2 * n + j, PAD:], ps, r[:, :], ALU.mult))

            def take_gate_tile(m, l):
                tile_done(U_GATE + m // 2, F_GATE + m // 2, l, m % 2)
                dve.tensor_tensor(gates[:, m, :], bank[m % 2][:, 0:T], r[:, :], ALU.mult).then_inc(tile_read, 1)

            def step0(n, l, ins):
                ins.then_inc(s0_step, 1)
                dve.wait_ge(s0_step, l * S0_STEPS + n)

            p0 = s0[0:META, :, 0:META]

            def softmax0_shift(l):
                dve.wait_ge(s0_done, l + 1)
                dve.wait_ge(consts, l + 2)
                for side in range(2):
                    ps = (o_bank, small)[side][0:META, 0:HEADS // 2 * META].rearrange("p (c k) -> p c k", k=META)
                    last = dve.tensor_tensor(s0[0:META, side::2, 0:META], ps, causal0[:, side::2, :], ALU.add)
                step0(1, l, last)
                step0(2, l, dve.reduce_max(stats0[:, 0, :], p0, AX_X))
                step0(3, l, dve.tensor_tensor(stats0[:, 0, :], stats0[:, 0, :], sink_cur[0:META, :], ALU.max))
                step0(4, l, dve.tensor_tensor(stats0[:, 1, :], sink_cur[0:META, :], stats0[:, 0, :], ALU.subtract))
                step0(5, l, dve.tensor_tensor(p0, p0, stats0[:, 0, :].unsqueeze(2).to_broadcast([META, HEADS, META]),
                                              ALU.subtract))

            def softmax0_end(l):
                dve.wait_ge(s0_exp, l + 1)
                step0(6, l, dve.reduce_sum(stats0[:, 3, :], p0, AX_X))
                step0(7, l, dve.tensor_tensor(stats0[:, 3, :], stats0[:, 3, :], stats0[:, 2, :], ALU.add))
                step0(8, l, dve.reciprocal(stats0[:, 3, :], stats0[:, 3, :]))
                step0(9, l, dve.tensor_tensor(p0, p0, stats0[:, 3, :].unsqueeze(2).to_broadcast([META, HEADS, META]),
                                              ALU.mult))
                step0(10, l, dve.transpose(p0T[:, :, :].rearrange("p h k -> p (h k)"),
                                           s0[:, :, :].rearrange("p h k -> p (h k)")))

            def bias_and_max(i, l):
                s, st = s_buf[:, i % 3, :], stats[:, i % 3, :]
                n = l * HEADS + i + 1
                dve.wait_ge(score_done, n)
                if i >= 3:
                    dve.wait_ge(pT_done, n - 3)
                dve.scalar_tensor_tensor(out=s, in0=distance, scalar=-slopes()[head_at(i)],
                                         in1=score_bank[i % 2][:, 0:BAND], op0=ALU.mult, op1=ALU.add
                                         ).then_inc(biased, 1)
                dve.wait_ge(biased, n)
                dve.reduce_max(st[:, 0:1], s[:, 0:T], AX_X)
                dve.reduce_max(st[:, 1:2], s[:, T:BAND], AX_X).then_inc(row_max, 1)
                dve.wait_ge(row_max, n)
                dve.tensor_scalar(st[:, 2:4], st[:, 0:2], sink_cur[:, i:i + 1], -1.0, ALU.max, ALU.mult
                                  ).then_inc(neg_max, 1)

            def invert_sum(i, l):
                st = stats[:, i % 3, :]
                n = l * HEADS + i + 1
                dve.wait_ge(exp_done, n)
                dve.tensor_tensor(st[:, 4:6], st[:, 4:6], st[:, 6:8], ALU.add).then_inc(den_ready, 1)
                dve.wait_ge(den_ready, n)
                dve.reciprocal(st[:, 0:2], st[:, 4:6]).then_inc(inv_ready, 1)

            def take_o(c, l):
                dve.wait_ge(o_done, l * HEADS + 2 * c + 2)
                dve.tensor_copy(o_hi[:, c, :], o_bank[:, 0:T]).then_inc(ohi_ready, 1)
                dve.wait_ge(ohi_ready, l * KD + c + 1)
                dve.tensor_tensor(o_lo[:, c, :], o_bank[:, 0:T], o_hi[:, c, :].bitcast(F32), ALU.subtract
                                  ).then_inc(olo_ready, 1)

            def mix(g, l):
                dve.wait_ge(win_done, l * GROUPS + g + 1)
                dve.scalar_tensor_tensor(out=pool_u[:, g, PAD:], in0=win[:, g % 2, PAD:],
                                         scalar=1.0 / POOL_WINDOWS[g], in1=pool_u[:, g, PAD:],
                                         op0=ALU.mult, op1=ALU.subtract).then_inc(mixed_ready, 1)

            def take_z(g, l):
                dve.wait_ge(grp_done, l * GROUPS + g + 1)
                ps = small[:, S_BC:S_BC + T]
                dve.tensor_scalar(z_hi[:, g, :], ps, scale_cur[:, g:g + 1], None, ALU.mult).then_inc(zhi_ready, 1)
                dve.wait_ge(zhi_ready, l * GROUPS + g + 1)
                dve.scalar_tensor_tensor(out=z_lo[:, g, :], in0=ps, scalar=scale_cur[:, g:g + 1],
                                         in1=z_hi[:, g, :].bitcast(F32), op0=ALU.mult, op1=ALU.subtract
                                         ).then_inc(zlo_ready, 1)

            def gated(first_gate, n, u, fin, l):
                b = 2 * (n % 2)
                dve.wait_ge(tanh_done, l * 2 * KD + first_gate + 2 * n + 2)

                def how(j, ps):
                    g = gates[:, first_gate + 2 * n + j, :]
                    return dve.scalar_tensor_tensor(out=g, in0=g, scalar=1.0, in1=ps, op0=ALU.add, op1=ALU.mult)

                take(u, fin, l, (b, b + 1), how)

            def merge_lo(m, l):
                dve.wait_ge(xhi_ready, l * 4 * KD + 2 * KD + m + 1)
                dve.scalar_tensor_tensor(out=x_lo[:, m, :], in0=gates[:, m, :], scalar=0.5,
                                         in1=x_hi[:, m, :].bitcast(F32), op0=ALU.mult, op1=ALU.subtract
                                         ).then_inc(xlo_ready, 1)

            dve.wait_ge(first_T, 1)
            dve.tensor_copy(g_all[:, :], small[:, 0:n_rows]).then_inc(rows_read, 1)
            for k in range(KD):
                dve.wait_ge(first_T, k + 2)
                dve.tensor_copy(h[:, k, :], bank[k % 4][:, 0:T]).then_inc(h_ready, 1)
            dve.wait_ge(rows_read, 1)

            with dve.Fori(0, DEPTH) as l:
                layer_columns(l)
                for u in range(3):
                    split_lo(u, l)
                for k in range(KD):
                    x_low(0, l, k)
                ffn(0, l)
                boundary(0, l)
                split_lo(41, l)
                mean_square(2, l)
                take_rms(2, l)
                rms_in(2, l)
                take(U_K, F_KV, l, (0, 1), lambda j, ps: dve.tensor_tensor(kT[:, j, :], ps, r[:, :], ALU.mult))
                take(U_V, F_KV + 1, l, (2, 3), lambda j, ps: dve.tensor_tensor(vT[:, j, :], ps, r[:, :], ALU.mult))
                split_lo(42, l)
                split_lo(43, l)
                for n in range(4):
                    take_q(n, l)
                    split_lo(44 + n, l)
                take_pool(0, l)
                softmax0_shift(l)
                split_lo(48, l)
                take_pool(1, l)
                for i in range(HEADS + 4):
                    if i < HEADS:
                        bias_and_max(i, l)
                    if 1 <= i <= HEADS:
                        invert_sum(i - 1, l)
                    if i < HEADS:
                        take_gate_tile(i, l)
                    if i % 2 == 0 and i < HEADS:
                        split_lo(49 + i // 2, l)
                    if i == 0:
                        softmax0_end(l)
                    if HEADS <= i < HEADS + 3:
                        split_lo(57 + i - HEADS, l)
                        if i > HEADS:
                            n = i - HEADS - 1
                            gated(0, n, U_PP + n, F_PP + n, l)
                    if i >= 5 and i % 2 == 1:
                        take_o((i - 5) // 2, l)
                    if i in MIX_STEPS:
                        mix(MIX_STEPS.index(i), l)
                    if i - 1 in GROUP_STEPS:
                        take_z(GROUP_STEPS.index(i - 1), l)
                gated(0, 2, U_PP + 2, F_PP + 2, l)
                split_lo(60, l)
                gated(0, 3, U_PP + 3, F_PP + 3, l)
                for n in range(4):
                    split_lo(61 + n, l)
                    gated(KD, n, U_AP + n, F_AP + n, l)
                    if n >= 1:
                        merge_lo(2 * n - 2, l)
                        merge_lo(2 * n - 1, l)
                merge_lo(6, l)
                merge_lo(7, l)
                split_lo(65, l)

                def take_y(n):
                    b = 2 * (n % 2)
                    take(U_WO + n, F_WO + n, l, (b, b + 1), lambda j, ps: dve.tensor_copy(y[:, 2 * n + j, :], ps))

                take_y(0)
                take_y(1)
                split_lo(66, l)
                split_lo(67, l)
                take_y(2)
                split_lo(68, l)
                take_y(3)
                boundary(1, l)
                ffn(1, l)
                boundary(2, l)

            for n in range(4):
                dve.wait_ge(final_T, n + 1)
                dve.tensor_copy(out_sb[:, n // 2, (n % 2) * 512:(n % 2 + 1) * 512], bank[n][:, :]).then_inc(out_ready, 1)

        @block.gpsimd
        def _(pool):
            pool.sem_inc(hf_ready, 2)
            pool.memset(ident[:, :], 0.0).then_inc(win_step, 1)
            pool.memset(half[:, :], -0.5)
            pool.memset(var[:, :], 1.0)
            pool.memset(ones[:, :], 1.0)
            pool.wait_ge(win_step, 1)
            pool.affine_select(out=ident[:, :], in_=ident[:, :], compare_op=ALU.not_equal, fill=1.0, base=0,
                               pattern=[[-1, P]], channel_multiplier=1).then_inc(consts, 1)

            def add_squares(q, l):
                for m in range(1, KD - 1):
                    pool.wait_ge(sq_done, (l * NORMS + q) * KD + m + 1)
                    if m == 1:
                        pool.wait_ge(ssq_done, l * NORMS + q + 1)
                        pool.tensor_tensor(acc[:, :], sq[:, 0, :], sq[:, 1, :], ALU.add).then_inc(acc_done, 1)
                    else:
                        pool.wait_ge(acc_done, (l * NORMS + q) * (KD - 2) + m - 1)
                        pool.tensor_tensor(acc[:, :], acc[:, :], sq[:, m % 2, :], ALU.add).then_inc(acc_done, 1)

            def inverse_rms(q, l):
                pool.wait_ge(var_ready, l * NORMS + q + 1)
                pool.tensor_tensor(rt[:, 0:3], var[:, 0:3], half[:, 0:3], ALU.pow).then_inc(rt_ready, 1)

            def ffn(f, l):
                add_squares(4 * f, l)
                inverse_rms(4 * f, l)
                with pool.Fori(0, KF // 2) as i:
                    for j in range(2):
                        n = l * 2 * KF + f * KF + i * 2 + j
                        pool.wait_ge(silu_done, n + 3)
                        pool.wait_ge(tile_read, l * TILES + T_FFN_IN[f] + i * 4 + 3 + j)
                        pool.tensor_tensor(hid_hi[:, ds(i * 2 + j, 1), :].rearrange("p o t -> p (o t)"), silu[:, j, :],
                                           up_r[:, j, :], ALU.mult).then_inc(hid_hi_ready, 1)
                        pool.tensor_tensor(hid_f[:, j, :], silu[:, j, :], up_r[:, j, :], ALU.mult).then_inc(hf_ready, 1)
                        pool.wait_ge(hid_hi_ready, n + 1)
                        pool.wait_ge(hf_ready, n + 3)
                        pool.tensor_tensor(hid_lo[:, ds(i * 2 + j, 1), :].rearrange("p o t -> p (o t)"), hid_f[:, j, :],
                                           hid_hi[:, ds(i * 2 + j, 1), :].rearrange("p o t -> p (o t)").bitcast(F32),
                                           ALU.subtract).then_inc(hid_ready, 1)
                add_squares(4 * f + 1, l)
                inverse_rms(4 * f + 1, l)

            def window(g, l):
                done = sum(n + 2 for n in range(g))
                src, at = pool_u[:, g, :], 0
                for d in range(g + 1):
                    lag = 1 << d
                    dst = win[:, (2 * g - d) % 2, :]
                    a = at + lag
                    pool.tensor_tensor(dst[:, a:], src[:, a:], src[:, a - lag:PAD + T - lag], ALU.add
                                       ).then_inc(win_step, 1)
                    src, at = dst, a
                    pool.wait_ge(win_step, l * WIN_STEPS + done + d + 2)
                pool.tensor_tensor(src[:, PAD:2 * PAD], src[:, PAD:2 * PAD], ramp[:, g, :], ALU.mult
                                   ).then_inc(win_step, 1)
                pool.wait_ge(win_step, l * WIN_STEPS + done + g + 3)
                pool.sem_inc(win_done, 1)

            def normalise(i, l):
                s, st = s_buf[:, i % 3, :], stats[:, i % 3, :]
                pool.wait_ge(inv_ready, l * HEADS + i + 1)
                pool.tensor_tensor(s[:, 0:T], s[:, 0:T], st[:, 0:1].to_broadcast([P, T]), ALU.mult)
                pool.tensor_tensor(s[:, T:BAND], s[:, T:BAND], st[:, 1:2].to_broadcast([P, BAND - T]), ALU.mult
                                   ).then_inc(p_ready, 1)

            with pool.Fori(0, DEPTH) as l:
                ffn(0, l)
                add_squares(2, l)
                inverse_rms(2, l)
                pool.memset(pool_u[:, :, 0:PAD], 0.0)
                pool.memset(s0[:, :, :], 0.0).then_inc(consts, 1)
                pool.wait_ge(consts, l + 2)
                for i in range(HEADS + 1):
                    if i in WINDOW_STEPS:
                        g = WINDOW_STEPS.index(i)
                        pool.wait_ge(tile_read, l * TILES + T_POOL + g + 1)
                        if g >= 1:
                            pool.wait_ge(mixed_ready, l * GROUPS + g)
                        window(g, l)
                    if i >= 1:
                        normalise(i - 1, l)
                for m in range(KD):
                    pool.wait_ge(tile_read, l * TILES + T_AP + m + 1)
                    pool.tensor_tensor(gates[:, m, :], gates[:, m, :], gates[:, KD + m, :], ALU.add
                                       ).then_inc(merged, 1)
                add_squares(3, l)
                inverse_rms(3, l)
                ffn(1, l)


WINDOW_STEPS = (0, 2, 4, 6)
MIX_STEPS = (1, 3, 5, 7)
GROUP_STEPS = (3, 5, 7, 9)
S0_STEPS, S0_SHIFTED = 10, 5


def geometry_table():
    keys = np.arange(T)
    parts = []
    for first, n_keys in ((META + P, T), (META, META + P)):
        d = (first + np.arange(P))[:, None] - keys[None, :n_keys]
        parts.append(np.where(keys[None, :n_keys] < META, 0.0, np.where((d >= 0) & (d < WINDOW), d, FAR)))
    k = np.arange(META)
    mask = np.where(k[None, :] <= (np.arange(P)[:, None] % META), 0.0, -1e30)
    parts.append(np.tile(mask, (1, HEADS)))
    t = np.arange(PAD) + 1
    parts.append(np.tile(np.concatenate([w / np.minimum(t, w) for w in POOL_WINDOWS])[None], (P, 1)))
    return np.concatenate(parts, axis=1).astype(np.float32)


_INS = ["x", "meta_tokens", "norm_g", "ffn_w_in", "ffn_w_out", "w_in", "pool_w_grp", "pool_scale",
        "w_pool_proj", "sinks", "w_attn_proj", "w_o"]


def kernel(**inputs):
    import concourse.bacc as bacc
    from concourse.bass_utils import run_bass_kernel_spmd

    nc = bacc.Bacc("TRN2", target_bir_lowering=False, num_devices=1)
    arrays, args = {}, []
    for name in _INS + ["geometry"]:
        a = geometry_table() if name == "geometry" else np.ascontiguousarray(inputs[name])
        arrays[f"in_{name}"] = a
        args.append(nc.dram_tensor(f"in_{name}", a.shape, F32, kind="ExternalInput").ap())
    args.append(nc.dram_tensor("out_h", (1, SEQ, D), F32, kind="ExternalOutput").ap())
    trunk(nc, *args)
    result = run_bass_kernel_spmd(nc, [arrays], core_ids=[0])
    return result.results[0]["out_h"]
```

```python
from contextlib import ExitStack

import numpy as np
import concourse.bass as bass
from concourse import mybir

F32 = mybir.dt.float32
F32R = mybir.dt.float32r
ALU = mybir.AluOpType
ACT = mybir.ActivationFunctionType
AX_X = mybir.AxisListType.X
ds = bass.ds

P = 128
D = 1024
SEQ = 256
META = 16
T = META + SEQ
DEPTH = 2
HEADS, KV_HEADS, DH = 16, 4, 64
WINDOW = 128
POOL_WINDOWS = (2, 4, 8, 16)
GROUPS = len(POOL_WINDOWS)
POOL_DIM = GROUPS * P
Q_DIM = HEADS * DH
KV_DIM = KV_HEADS * DH
FF = ((8 * D // 3 + 127) // 128) * 128
EPS = 1e-6
KD = D // P
KF = FF // P
UW = 2 * P
RING = 4
OUT_K = (6, 5, 6, 5)
OUT_K0 = (0, 6, 11, 17)
B1, B2 = slice(META, META + P), slice(META + P, T)
BAND = T + META + P
FAR = 1e33
PAD = POOL_WINDOWS[-1]

U_FFN_IN = (0, 66)
U_FFN_OUT = (22, 88)
U_K, U_V, U_Q, U_POOL, U_GATE, U_PP, U_AP, U_WO = 38, 39, 40, 44, 46, 54, 58, 62
UNITS = 104
N_IN, N_OUT = FF * 2 // UW, 16
assert N_IN == 22 and sum(OUT_K) == KF and UNITS % RING == 0
T_FFN_IN, T_FFN_OUT = (0, 108), (44, 152)
T_KV, T_Q, T_POOL, T_GATE, T_PP, T_AP, T_WO = 52, 56, 64, 68, 84, 92, 100
TILES = 160
F_FFN_IN, F_FFN_OUT = (0, 54), (22, 76)
F_KV, F_Q, F_POOL, F_GATE, F_PP, F_AP, F_WO = 26, 28, 32, 34, 42, 46, 50
FINISHERS = 80
FFN_LAG = 8
TR0 = FFN_LAG - 4
NORMS = 6


def slopes():
    return [2.0 ** (-8.0 * (h + 1) / HEADS) for h in range(HEADS)]


def head_at(i):
    tile, side = divmod(i, 2)
    group, t = divmod(tile, 4)
    return 8 * group + 4 * side + t


def kv_at(i):
    tile, side = divmod(i, 2)
    return 2 * (tile // 4) + side


def unit_k(u):
    for first in U_FFN_OUT:
        if first <= u < first + N_OUT:
            return OUT_K[(u - first) % 4]
    return GROUPS if U_PP <= u < U_AP else KD


def unit_dmas(u):
    return 2 if U_Q <= u < U_POOL else 4 if U_AP <= u < U_WO else 1


SLOT_DMAS = [sum(unit_dmas(u) for u in range(s, UNITS, RING)) for s in range(RING)]


def landed_at(u, layer, more=0):
    upto = sum(unit_dmas(v) for v in range(u % RING, u + 1, RING))
    return (layer * SLOT_DMAS[u % RING] + upto + more) * 16


def trunk(nc, x, meta_tokens, norm_g, ffn_w_in, ffn_w_out, w_in, pool_w_grp, pool_scale, w_pool_proj,
          sinks, w_attn_proj, w_o, geometry, out):
    with ExitStack() as ctx:
        def sb(name, shape, dt=F32):
            return ctx.enter_context(nc.sbuf_tensor(name, shape, dt))

        def sem(name):
            return ctx.enter_context(nc.semaphore(name))

        raw = sb("raw", [P, RING, KD * UW])
        w_hi = sb("w_hi", [P, RING, KD * UW], F32R)
        w_lo = sb("w_lo", [P, RING, KD * UW], F32R)
        h = sb("h", [P, KD, T])
        x_hi = sb("x_hi", [P, KD, T], F32R)
        x_lo = sb("x_lo", [P, KD, T], F32R)
        y = sb("y", [P, KD, T])
        sq = sb("sq", [P, 2, T])
        acc = sb("acc", [P, T])
        r = sb("r", [P, T])
        tmp = sb("tmp", [P, 2, PAD + T])
        var = sb("var", [P, 4])
        rt = sb("rt", [P, 4])
        half = sb("half", [P, 4])
        ident = sb("ident", [P, P])
        ones = sb("ones", [P, 1])
        g_all = sb("g_all", [P, DEPTH * NORMS * KD + DEPTH * GROUPS])
        g_cur = sb("g_cur", [P, NORMS * KD])
        g_next = sb("g_next", [P, KD])
        scale_cur = sb("scale_cur", [P, GROUPS])
        sink_all = sb("sink_all", [P, DEPTH * HEADS])
        sink_cur = sb("sink_cur", [P, HEADS])
        geo = sb("geo", [P, BAND + HEADS * META + GROUPS * PAD])
        distance = geo[:, 0:BAND]
        causal0 = geo[0:META, BAND:BAND + HEADS * META].rearrange("p (h k) -> p h k", h=HEADS)
        ramp = geo[:, BAND + HEADS * META:].rearrange("p (g t) -> p g t", g=GROUPS)

        def shared_sizes(items):
            return sum(-(-int(np.prod(s[1:])) * 4 // 32) * 32 for _, s, _ in items)

        ffn_items = [("hid_hi", [P, KF, T], F32R), ("hid_lo", [P, KF, T], F32R), ("gate_r", [P, 2, T], F32),
                     ("silu", [P, 2, T], F32), ("up_r", [P, 2, T], F32), ("hid_f", [P, 2, T], F32)]
        mix_items = [("kT", [P, 2, T], F32), ("v_tok", [P, 2, KV_DIM], F32), ("v_meta", [META, KV_DIM], F32),
                     ("gates", [P, 2 * KD, T], F32), ("pool_u", [P, GROUPS, PAD + T], F32),
                     ("z_hi", [P, GROUPS, T], F32R),
                     ("z_lo", [P, GROUPS, T], F32R), ("o_hi", [P, KD, T], F32R), ("o_lo", [P, KD, T], F32R),
                     ("s", [P, 3, BAND], F32), ("pT", [P, 2, 3 * P], F32), ("pT_meta", [META, 2, 2 * P], F32),
                     ("s0", [32, HEADS, 32], F32), ("stats0", [META, 4, HEADS], F32),
                     ("stats", [P, 3, 8], F32), ("w_grp", [P, GROUPS, P], F32)]
        arena_bytes = max(shared_sizes(ffn_items), shared_sizes(mix_items))
        arena = sb("arena", [P, arena_bytes // 4])
        base = nc.sbuf_base - arena_bytes

        def place(items):
            at, placed = base, []
            for name, shape, dt in items:
                placed.append(nc.alloc_sbuf_tensor_at(name, shape, dt, offset=at))
                at += shared_sizes([(name, shape, dt)])
            return placed

        hid_hi, hid_lo, gate_r, silu, up_r, hid_f = place(ffn_items)
        (kT, v_tok, v_meta, gates, pool_u, z_hi, z_lo, o_hi, o_lo, s_buf, pT, pT_meta, s0, stats0,
         stats, w_grp) = place(mix_items)
        win = tmp
        p0T = sq[0:32].rearrange("p a t -> p (a t)")[:, 0:HEADS * 32].rearrange("p (h k) -> p h k", h=HEADS)
        qT = y
        vT = gates[:, 2 * KD - 2:2 * KD, :]
        first_x = gates[:, 0:8, :].rearrange("p a t -> p (a t)")[:, 0:2 * D].rearrange("p (b d) -> p b d", b=2)
        first_meta = gates[0:META, 8:12, :].rearrange("p a t -> p (a t)")[:, 0:D]
        n_rows = DEPTH * NORMS * KD + DEPTH * GROUPS
        first_rows = gates[0:n_rows, 12, 0:P]
        out_sb = gates[:, 0:8, :].rearrange("p a t -> p (a t)")[:, 0:2 * D].rearrange("p (b d) -> p b d", b=2)

        bank = [ctx.enter_context(nc.psum_tensor(f"bank{b}", [P, 512], F32)) for b in range(8)]
        score_bank = (bank[2], bank[3])
        pT_bank, pTm_bank, o_bank, small = bank[4], bank[5], bank[6], bank[7]
        warm = o_bank
        S_SUM, S_BC = 0, 128

        inputs_in = sem("inputs_in")
        geo_in = sem("geo_in")
        raw_landed = [sem(f"raw_landed{s}") for s in range(RING)]
        w_grp_in = sem("w_grp_in")
        out_stored = sem("out_stored")
        consts = sem("consts")
        hi_done = sem("hi_done")
        lo_done = sem("lo_done")
        unit_done = sem("unit_done")
        first_done = sem("first_done")
        tile_read = sem("tile_read")
        layer_consts = sem("layer_consts")
        first_T = sem("first_T")
        rows_read = sem("rows_read")
        h_ready = sem("h_ready")
        t_ready = sem("t_ready")
        xhi_ready = sem("xhi_ready")
        xlo_ready = sem("xlo_ready")
        sq_done = sem("sq_done")
        acc_done = sem("acc_done")
        ssq_done = sem("ssq_done")
        var_ready = sem("var_ready")
        rt_ready = sem("rt_ready")
        bcast_done = sem("bcast_done")
        r_ready = sem("r_ready")
        silu_done = sem("silu_done")
        hf_ready = sem("hf_ready")
        hid_hi_ready = sem("hid_hi_ready")
        hid_ready = sem("hid_ready")
        v_turned = sem("v_turned")
        v_ready = sem("v_ready")
        s0_done = sem("s0_done")
        s0_step = sem("s0_step")
        s0_exp = sem("s0_exp")
        score_done = sem("score_done")
        biased = sem("biased")
        row_max = sem("row_max")
        neg_max = sem("neg_max")
        exp_done = sem("exp_done")
        den_ready = sem("den_ready")
        inv_ready = sem("inv_ready")
        p_ready = sem("p_ready")
        pT_done = sem("pT_done")
        pT_ready = sem("pT_ready")
        o_done = sem("o_done")
        ohi_ready = sem("ohi_ready")
        olo_ready = sem("olo_ready")
        tanh_done = sem("tanh_done")
        win_step = sem("win_step")
        win_done = sem("win_done")
        mixed_ready = sem("mixed_ready")
        grp_done = sem("grp_done")
        zhi_ready = sem("zhi_ready")
        zlo_ready = sem("zlo_ready")
        merged = sem("merged")
        final_T = sem("final_T")
        out_ready = sem("out_ready")
        out_late = sem("out_late")

        def split_parts(u, halves=False):
            s, n = u % RING, unit_k(u) * UW
            if not U_Q <= u < U_POOL:
                cuts = (0, n // 2, n) if halves else (0, n)
                return [(raw[:, s, a:b], w_hi[:, s, a:b], w_lo[:, s, a:b]) for a, b in zip(cuts, cuts[1:])]
            from_raw = raw[:, s, :].rearrange("p (k s t c) -> p t k s c", s=2, t=2, c=DH)
            to_hi, to_lo = (w[:, s, :].rearrange("p (k t s c) -> p t k s c", s=2, t=2, c=DH) for w in (w_hi, w_lo))
            return [(from_raw[:, t], to_hi[:, t], to_lo[:, t]) for t in range(2)]

        block = ctx.enter_context(nc.Block())

        WIN_STEPS = sum(g + 2 for g in range(GROUPS))

        @block.sync
        def _(sp):
            sp.dma_start(first_x, x[0].rearrange("(b p) d -> p b d", b=2)).then_inc(inputs_in, 16)
            sp.dma_start(first_meta, meta_tokens).then_inc(inputs_in, 16)
            sp.dma_start(first_rows[0:DEPTH * NORMS * KD, :], norm_g.rearrange("l n (k p) -> (l n k) p", p=P)
                         ).then_inc(inputs_in, 16)
            sp.dma_start(first_rows[DEPTH * NORMS * KD:n_rows, :], pool_scale.rearrange("l (g p) -> (l g) p", p=P)
                         ).then_inc(inputs_in, 16)

            def slot_free(u, l, more=0):
                sp.wait_ge(lo_done, l * UNITS + u + 1 + more)

            def load(u, src, dst=None):
                s = u % RING
                to = raw[:, s, 0:unit_k(u) * UW].rearrange("p (k c) -> p k c", c=UW) if dst is None else dst
                sp.dma_start(to, src).then_inc(raw_landed[s], 16)

            def ffn_loads(l, f):
                w1 = ffn_w_in[ds(l, 1), f].rearrange("o (k p) n -> p (o k) n", p=P)
                w2 = ffn_w_out[ds(l, 1), f].rearrange("o (k p) n -> p (o k) n", p=P)
                u0 = U_FFN_IN[f]
                for j in range(2):
                    slot_free(u0 + j, l)
                    load(u0 + j, w1[:, :, j * FF:j * FF + UW])
                with sp.Fori(0, N_IN - 5, 4) as i:
                    for j in range(4):
                        slot_free(u0 + 2 + j, l, i)
                        load(u0 + 2 + j, w1[:, :, ds(i * (UW // 2) + (UW * (1 + j // 2) + j % 2 * FF), UW)])
                u0 = U_FFN_OUT[f]
                with sp.Fori(0, N_OUT - 3, 4) as i:
                    for j in range(4):
                        slot_free(u0 + j, l, i)
                        load(u0 + j, w2[:, OUT_K0[j]:OUT_K0[j] + OUT_K[j], ds(i * (UW // 4), UW)])

            with sp.Fori(0, DEPTH) as l:
                ffn_loads(l, 0)
                w = w_in[ds(l, 1)].rearrange("o (k p) n -> p (o k) n", p=P)
                q0, k0 = POOL_DIM, POOL_DIM + Q_DIM
                v0, g0 = k0 + KV_DIM, k0 + 2 * KV_DIM
                for u in range(U_K, U_PP):
                    slot_free(u, l)
                    if u == U_POOL:
                        sp.wait_ge(unit_done, l * UNITS + U_K + RING)
                        sp.dma_start(w_grp[:, :, :], pool_w_grp[ds(l, 1)].rearrange("o g c d -> c (o g) d")
                                     ).then_inc(w_grp_in, 16)
                    if U_Q <= u < U_POOL:
                        c = q0 + (8 * ((u - U_Q) // 2) + 2 * ((u - U_Q) % 2)) * DH
                        to = raw[:, u % RING, :].rearrange("p (k s c) -> p k s c", s=2, c=P)
                        for side in range(2):
                            load(u, w[:, :, c + side * 4 * DH:c + side * 4 * DH + P], to[:, :, side, :])
                    else:
                        c = (k0 if u == U_K else v0 if u == U_V else (u - U_POOL) * UW if u < U_GATE
                             else g0 + (u - U_GATE) * UW)
                        load(u, w[:, :, c:c + UW])
                wp = w_pool_proj[ds(l, 1)].rearrange("o (k p) n -> p (o k) n", p=P)
                for m in range(4):
                    slot_free(U_PP + m, l)
                    load(U_PP + m, wp[:, :, m * UW:(m + 1) * UW])
                wa = w_attn_proj[ds(l, 1)].rearrange("o (g s t f) n -> g s f (o t) n", g=2, s=2, t=4)
                for m in range(4):
                    u = U_AP + m
                    slot_free(u, l)
                    to = raw[:, u % RING, :].rearrange("p (g t c) -> p g t c", g=2, t=4)
                    for g in range(2):
                        for side in range(2):
                            load(u, wa[g, side, :, :, m * UW:(m + 1) * UW], to[side * DH:(side + 1) * DH, g])
                wo = w_o[ds(l, 1)].rearrange("o (k p) n -> p (o k) n", p=P)
                for m in range(4):
                    slot_free(U_WO + m, l)
                    load(U_WO + m, wo[:, :, m * UW:(m + 1) * UW])
                ffn_loads(l, 1)

            for half_d in range(2):
                for b in range(2):
                    if half_d == 1 and b == 1:
                        sp.wait_ge(out_late, 1)
                    else:
                        sp.wait_ge(out_ready, 2 * half_d + b + 1)
                    c = slice(half_d * (D // 2), (half_d + 1) * (D // 2))
                    sp.dma_start(out[0, b * P:(b + 1) * P, c], out_sb[:, b, c]).then_inc(out_stored, 16)
            sp.wait_ge(out_stored, 16 * 4)

        @block.tensor
        def _(pe):
            pe.sem_inc(unit_done, RING)
            pe.sem_inc(ssq_done, 1)

            def weights(u, k, mt):
                s = u % RING
                return [w[:, s, k * UW + mt * P:k * UW + (mt + 1) * P] for w in (w_hi, w_lo)]

            def products(ps, w, a_hi, a_lo, start, stop, t0):
                pe.matmul(ps[:, t0:T], w[0], a_hi[:, t0:T], start=start, stop=False)
                pe.matmul(ps[:, t0:T], w[0], a_lo[:, t0:T], start=False, stop=False)
                return pe.matmul(ps[:, t0:T], w[1], a_hi[:, t0:T], start=False, stop=stop)

            def unit_split(u, l, more=0):
                pe.wait_ge(lo_done, l * UNITS + u + RING + 1 + more)

            def tile_free(t, l, lag, more=0):
                pe.wait_ge(tile_read, l * TILES + t - lag + 1 + TR0 + more)

            def deep_pair(u, l, a_hi, a_lo, operand_ready, extra=None, t=None, t0=0):
                unit_split(u, l)
                unit_split(u + 1, l)
                for k in range(KD):
                    operand_ready(k)
                    for c in range(4):
                        if k == 0 and t is not None:
                            tile_free(t + c, l, 4)
                        if k == KD - 1 and c == 0 and extra is not None:
                            extra()
                        last = products(bank[c], weights(u + c // 2, k, c % 2), a_hi[:, k, :], a_lo[:, k, :],
                                        k == 0, k == KD - 1, t0)
                        if k == KD - 1:
                            last.then_inc(first_done if c % 2 == 0 else unit_done, 1)

            def unit_tile(u, l, mt, b, nk, a_hi, a_lo, t0=0):
                for k in range(nk):
                    last = products(bank[b], weights(u, k, mt), a_hi[:, k, :], a_lo[:, k, :], k == 0, k == nk - 1, t0)
                last.then_inc(first_done if mt == 0 else unit_done, 1)

            def unit(u, l, t, banks, lag, nk, a_hi, a_lo, more=0, more_t=0, t0=0):
                unit_split(u, l, more)
                for mt in range(2):
                    tile_free(t + mt, l, lag, more_t)
                    unit_tile(u, l, mt, banks[mt], nk, a_hi, a_lo, t0)

            def sum_squares(q, l):
                n = l * NORMS + q
                if q % 2 == 1:
                    pe.wait_ge(r_ready, l * 3 + q // 2 + 1)
                for part in range(3):
                    if part == 0:
                        pe.wait_ge(acc_done, (n + 1) * (KD - 3))
                    else:
                        pe.wait_ge(sq_done, (n + 1) * KD + part - 2)
                    src = acc[:, :] if part == 0 else sq[:, part - 1, :]
                    for b in range(3):
                        m = min(P, T - b * P)
                        last = pe.matmul(small[0:m, S_SUM + b:S_SUM + b + 1], src[:, b * P:b * P + m], ones[:, 0:1],
                                         start=(part == 0 and b == 0), stop=(part == 2), skip_group_check=True)
                last.then_inc(ssq_done, 1)

            def keep_warm(n):
                for _ in range(n):
                    pe.matmul(warm[:, 0:P], ident[:, :], ident[:, :], start=True, stop=True)

            def spread_rms(q, l):
                pe.wait_ge(rt_ready, l * NORMS + q + 1)
                for b in range(3):
                    n = min(P, T - b * P)
                    last = pe.matmul(small[:, S_BC + b * P:S_BC + b * P + n], rt[0:n, b:b + 1].to_broadcast([n, P]),
                                     ident[0:n, 0:n], start=True, stop=True)
                last.then_inc(bcast_done, 1)

            def x_tile(n, l):
                pe.wait_ge(xlo_ready, l * 4 * KD + n + 1)

            def ffn(f, l, t0=0):
                u0, tile0 = U_FFN_IN[f], T_FFN_IN[f]
                deep_pair(u0, l, x_hi, x_lo, lambda k: x_tile((0, 3 * KD)[f] + k, l), lambda: sum_squares(4 * f, l), t0=t0)
                spread_rms(4 * f, l)
                with pe.Fori(0, (N_IN - 2) // 4) as i:
                    for j in range(4):
                        banks, lag = (((4, 5), FFN_LAG), ((2, 3), 4), ((0, 1), FFN_LAG), ((2, 3), 4))[j]
                        unit(u0 + 2 + j, l, tile0 + 4 + 2 * j, banks, lag, KD, x_hi, x_lo, i * 4, i * 8, t0)
                u0, tile0 = U_FFN_OUT[f], T_FFN_OUT[f]
                with pe.Fori(0, N_OUT // 4) as i:
                    for j in range(4):
                        unit_split(u0 + j, l, i * 4)
                        pe.wait_ge(hid_ready, l * 2 * KF + f * KF + OUT_K0[j] + OUT_K[j])
                        for mt in range(2):
                            if j == 0:
                                tile_free(tile0 + mt, l, 2, i * 2)
                            for k in range(OUT_K[j]):
                                kk = OUT_K0[j] + k
                                last = products(bank[mt], weights(u0 + j, k, mt), hid_hi[:, kk, :], hid_lo[:, kk, :],
                                                kk == 0, kk == KF - 1, t0)
                            if mt == 0 and j == 3:
                                last.then_inc(first_done, 1)
                        last.then_inc(unit_done, 1)
                sum_squares(4 * f + 1, l)
                keep_warm(WARM_RMS)
                spread_rms(4 * f + 1, l)
                keep_warm(WARM_X)

            def turn_v():
                for j in range(2):
                    for b, blk in enumerate((B1, B2)):
                        pe.transpose(pT_bank[:, b * KV_DIM + j * P:b * KV_DIM + (j + 1) * P], vT[:, j, blk], ident[:, :])
                for j in range(2):
                    last = pe.transpose(pTm_bank[:, j * P:(j + 1) * P], vT[:, j, 0:P], ident[:, :])
                last.then_inc(v_turned, 1)

            def rows(i):
                return slice((i % 2) * DH, (i % 2) * DH + DH)

            def scores0(l):
                for i in range(HEADS):
                    last = pe.matmul((o_bank, small)[i % 2][0:META, i // 2 * META:(i // 2 + 1) * META], qT[rows(i), i // 2, 0:META],
                                     kT[rows(i), i // 8, 0:META], start=True, stop=True)
                last.then_inc(s0_done, 1)

            def scores(i, l):
                if i >= 2:
                    pe.wait_ge(biased, l * HEADS + i - 1)
                sc = score_bank[i % 2]
                pe.matmul(sc[:, 0:T], qT[rows(i), i // 2, B2], kT[rows(i), i // 8, 0:T], start=True, stop=True)
                pe.matmul(sc[:, T:BAND], qT[rows(i), i // 2, B1], kT[rows(i), i // 8, 0:META + P], start=True,
                          stop=True).then_inc(score_done, 1)

            def turn_p(i, l):
                pe.wait_ge(p_ready, l * HEADS + i + 1)
                if i >= 1:
                    pe.wait_ge(pT_ready, l * HEADS + i)
                s = s_buf[:, i % 3, :]
                pe.transpose(pT_bank[:, 0:P], s[:, T + META:BAND], ident[:, :])
                pe.transpose(pT_bank[:, P:2 * P], s[:, META:META + P], ident[:, :])
                pe.transpose(pT_bank[:, 2 * P:3 * P], s[:, META + P:T], ident[:, :])
                pe.transpose(pTm_bank[:, 0:P], s[:, T:T + P], ident[:, :])
                pe.transpose(pTm_bank[:, P:2 * P], s[:, 0:P], ident[:, :]).then_inc(pT_done, 1)

            def attend(i, l):
                pe.wait_ge(pT_ready, l * HEADS + i + 1)
                if i == 0:
                    pe.wait_ge(v_ready, 2 * l + 2)
                    pe.wait_ge(s0_step, (l + 1) * S0_STEPS)
                if i % 2 == 0 and i >= 2:
                    pe.wait_ge(olo_ready, l * KD + i // 2)
                o = o_bank[rows(i), :]
                c = slice(kv_at(i) * DH, (kv_at(i) + 1) * DH)
                pe.matmul(o[:, 0:META], v_meta[0:META, c], p0T[0:META, i, 0:META], start=True, stop=False,
                          skip_group_check=True)
                pe.matmul(o[:, META:T], v_meta[0:META, c], pT_meta[0:META, i % 2, :], start=False, stop=False,
                          skip_group_check=True)
                pe.matmul(o[:, META:T], v_tok[:, 0, c], pT[:, i % 2, 0:2 * P], start=False, stop=False,
                          skip_group_check=True)
                pe.matmul(o[:, META + P:T], v_tok[:, 1, c], pT[:, i % 2, 2 * P:3 * P], start=False, stop=True,
                          skip_group_check=True).then_inc(o_done, 1)

            def group(g, l):
                pe.wait_ge(mixed_ready, l * GROUPS + g + 1)
                if g == 0:
                    pe.wait_ge(w_grp_in, l * 16 + 16)
                    pe.wait_ge(r_ready, l * 3 + 2)
                else:
                    pe.wait_ge(zlo_ready, l * GROUPS + g)
                pe.matmul(small[:, S_BC:S_BC + T], w_grp[:, g, :], pool_u[:, g, PAD:], start=True, stop=True
                          ).then_inc(grp_done, 1)

            def after_kv(l, t0):
                for n in range(4):
                    unit(U_Q + n, l, T_Q + 2 * n, Q_BANKS[n], (8, 6, 4, 4)[n], KD, x_hi, x_lo, t0=t0)
                    if n == 2:
                        turn_v()
                unit(U_POOL, l, T_POOL, (2, 3), 2, KD, x_hi, x_lo)
                scores0(l)
                unit(U_POOL + 1, l, T_POOL + 2, (0, 1), 4, KD, x_hi, x_lo)
                for i in range(HEADS + 3):
                    if i < HEADS:
                        u, mt = U_GATE + i // 2, i % 2
                        if mt == 0:
                            unit_split(u, l)
                        tile_free(T_GATE + i, l, 2)
                        unit_tile(u, l, mt, mt, KD, x_hi, x_lo, t0)
                        scores(i, l)
                    if 2 <= i < HEADS + 2:
                        turn_p(i - 2, l)
                    if i >= 3:
                        attend(i - 3, l)
                    if i in GROUP_STEPS:
                        group(GROUP_STEPS.index(i), l)
                    if i >= HEADS:
                        m = i - HEADS
                        if m == 0:
                            pe.wait_ge(zlo_ready, (l + 1) * GROUPS)
                            pe.wait_ge(biased, (l + 1) * HEADS)
                        unit(U_PP + m, l, T_PP + 2 * m, (2 * (m % 2), 2 * (m % 2) + 1), 2 if m == 0 else 4,
                             GROUPS, z_hi, z_lo, t0=t0)
                unit(U_PP + 3, l, T_PP + 6, (2, 3), 4, GROUPS, z_hi, z_lo, t0=t0)
                pe.wait_ge(olo_ready, (l + 1) * KD)
                for m in range(4):
                    b = 2 * (m % 2)
                    unit(U_AP + m, l, T_AP + 2 * m, (b, b + 1), 4, KD, o_hi, o_lo, t0=t0)
                deep_pair(U_WO, l, x_hi, x_lo, lambda k: x_tile(2 * KD + k, l), t=T_WO, t0=t0)
                for m in range(2, 4):
                    b = 2 * (m % 2)
                    unit(U_WO + m, l, T_WO + 2 * m, (b, b + 1), 4, KD, x_hi, x_lo, t0=t0)
                sum_squares(3, l)
                keep_warm(WARM_RMS)
                spread_rms(3, l)
                keep_warm(WARM_X)
                ffn(1, l, t0)

            pe.wait_ge(inputs_in, 16 * 4)
            pe.wait_ge(consts, 1)
            pe.transpose(small[:, 0:n_rows], first_rows, ident[0:n_rows, 0:n_rows]).then_inc(first_T, 1)
            for k in range(KD):
                if k >= 4:
                    pe.wait_ge(h_ready, k - 3)
                b = bank[k % 4]
                pe.transpose(b[:, 0:META], first_meta[:, k * P:(k + 1) * P], ident[0:META, 0:META])
                pe.transpose(b[:, B1], first_x[:, 0, k * P:(k + 1) * P], ident[:, :])
                pe.transpose(b[:, B2], first_x[:, 1, k * P:(k + 1) * P], ident[:, :]).then_inc(first_T, 1)

            with pe.Fori(0, DEPTH) as l:
                ffn(0, l)
                deep_pair(U_K, l, x_hi, x_lo, lambda k: x_tile(KD + k, l), lambda: sum_squares(2, l))
                spread_rms(2, l)
                with pe.If(l < DEPTH - 1):
                    after_kv(l, 0)
                with pe.Else():
                    after_kv(l, META)

            for k in range(KD):
                pe.wait_ge(h_ready, KD * 3 * DEPTH + k + 1)
                if k == 0:
                    pe.wait_ge(tile_read, DEPTH * TILES + TR0)
                for b in range(2):
                    last = pe.transpose(bank[2 * b + k // 4][:, k % 4 * P:(k % 4 + 1) * P], h[:, k, (B1, B2)[b]], ident[:, :])
                    if k % 4 == 3:
                        last.then_inc(final_T, 1)

        @block.scalar
        def _(act):
            act.sem_inc(silu_done, 2)

            def split_hi(u, l, more=0):
                act.wait_ge(raw_landed[u % RING], landed_at(u, l, more))
                act.wait_ge(unit_done, l * UNITS + u + 1 + (more * 4))
                for w, hi, _ in split_parts(u):
                    last = act.activation(hi, w, ACT.Copy)
                last.then_inc(hi_done, 1)

            def square(n, m, src, ready, at):
                act.wait_ge(ready, at)
                if m < 2:
                    act.wait_ge(ssq_done, n + 1)
                else:
                    act.wait_ge(acc_done, n * (KD - 3) + max(1, m - 2))
                act.activation(sq[:, m % 2, :], src, ACT.Square).then_inc(sq_done, 1)

            def pre_norm(n, columns, h_before):
                for k in range(KD):
                    act.wait_ge(h_ready, h_before + k + 1)
                    act.activation(x_hi[:, k, :], h[:, k, :], ACT.Copy, scale=columns[:, k:k + 1]).then_inc(xhi_ready, 1)
                    square(n, k, h[:, k, :], h_ready, h_before + k + 1)

            def silus(f, l, pair, more=0):
                for j in range(2):
                    act.wait_ge(tile_read, l * TILES + T_FFN_IN[f] + 4 * pair + j + 1 + TR0 + more * 4)
                    act.wait_ge(hf_ready, l * 2 * KF + f * KF + 2 * pair + j + 1 + more * 2)
                    act.activation(silu[:, j, :], gate_r[:, j, :], ACT.Silu).then_inc(silu_done, 1)

            def ffn(f, l):
                u0 = U_FFN_IN[f]
                split_hi(u0 + 3, l)
                silus(f, l, 0)
                split_hi(u0 + 4, l)
                with act.Fori(0, 4) as i:
                    for j in range(4):
                        split_hi(u0 + 5 + j, l, i)
                        if j % 2 == 1:
                            silus(f, l, 1 + j // 2, i * 2)
                for j in range(18, 22):
                    split_hi(u0 + j + 3, l)
                    if j % 2 == 1:
                        silus(f, l, (j - 1) // 2)
                u0 = U_FFN_OUT[f]

                def out_squares(i):
                    for m in (2 * i, 2 * i + 1):
                        square(l * NORMS + 4 * f + 1, m, y[:, m, :], tile_read,
                               l * TILES + T_FFN_OUT[f] + m + 1 + TR0)

                for i in range(3):
                    for j in range(4):
                        split_hi(u0 + 3 + 4 * i + j, l)
                    out_squares(i)
                split_hi(u0 + 15, l)
                if f == 0:
                    split_hi(U_K, l)
                    split_hi(U_V, l)
                    split_hi(U_Q, l)
                    out_squares(3)
                else:
                    with act.If(l < DEPTH - 1):
                        split_hi(0, l + 1)
                        split_hi(1, l + 1)
                        split_hi(2, l + 1)
                    out_squares(3)

            def exps(i, l):
                act.wait_ge(neg_max, l * HEADS + i + 1)
                s, st = s_buf[:, i % 3, :], stats[:, i % 3, :]
                act.activation(s[:, 0:T], s[:, 0:T], ACT.Exp, bias=st[:, 2:3], accum_out=st[:, 4:5])
                act.activation(s[:, T:BAND], s[:, T:BAND], ACT.Exp, bias=st[:, 3:4], accum_out=st[:, 5:6])
                act.activation(st[:, 6:8], st[:, 2:4], ACT.Exp, bias=sink_cur[:, i:i + 1]).then_inc(exp_done, 1)

            def take_pT(i, l):
                act.wait_ge(pT_done, l * HEADS + i + 1)
                if i >= 2:
                    act.wait_ge(o_done, l * HEADS + i - 1)
                act.activation(pT[:, i % 2, :], pT_bank[:, 0:3 * P], ACT.Copy)
                act.activation(pT_meta[0:META, i % 2, :], pTm_bank[0:META, 0:2 * P], ACT.Copy).then_inc(pT_ready, 1)

            def tanh(m, l):
                act.wait_ge(tile_read, l * TILES + T_GATE + m + 1 + TR0)
                act.activation(gates[:, m, :], gates[:, m, :], ACT.Tanh, scale=0.5).then_inc(tanh_done, 1)

            def merge_hi(m, l):
                act.wait_ge(merged, l * KD + m + 1)
                act.activation(x_hi[:, m, :], gates[:, m, :], ACT.Copy, scale=0.5).then_inc(xhi_ready, 1)

            act.preload_act_table(ACT.Silu)
            split_hi(0, 0)
            split_hi(1, 0)
            act.dma_start(geo[:, :], geometry).then_inc(geo_in, 16)
            act.dma_start(sink_all[:, :], sinks.rearrange("(o l) h -> o (l h)", o=1).to_broadcast([P, DEPTH * HEADS])
                          ).then_inc(geo_in, 16)
            act.wait_ge(layer_consts, 1)
            pre_norm(0, g_next, 0)
            split_hi(2, 0)
            with act.Fori(0, DEPTH) as l:
                ffn(0, l)
                act.wait_ge(layer_consts, l + 2)
                pre_norm(l * NORMS + 2, g_cur[:, 2 * KD:3 * KD], l * 3 * KD + KD)
                act.preload_act_table(ACT.Exp)
                for u in range(41, 46):
                    split_hi(u, l)
                act.wait_ge(v_turned, l + 1)
                act.activation(v_tok[:, :, :], pT_bank[:, :].rearrange("p (b c) -> p b c", b=2), ACT.Copy
                               ).then_inc(v_ready, 1)
                act.activation(v_meta[:, :], pTm_bank[0:META, 0:KV_DIM], ACT.Copy).then_inc(v_ready, 1)
                for u in range(46, 49):
                    split_hi(u, l)
                for i in range(HEADS + 3):
                    if i == 0:
                        act.wait_ge(s0_step, l * S0_STEPS + S0_SHIFTED)
                        act.activation(s0[0:META, :, 0:META], s0[0:META, :, 0:META], ACT.Exp)
                        act.activation(stats0[:, 2, :], stats0[:, 1, :], ACT.Exp).then_inc(s0_exp, 1)
                    if 1 <= i <= HEADS:
                        tanh(i - 1, l)
                    if i % 2 == 0 and i < HEADS:
                        split_hi(49 + i // 2, l)
                    if i >= HEADS:
                        split_hi(57 + i - HEADS, l)
                    if 2 <= i < HEADS + 2:
                        take_pT(i - 2, l)
                    if i < HEADS:
                        exps(i, l)
                split_hi(60, l)
                for n in range(4):
                    split_hi(61 + n, l)
                    if n >= 1:
                        merge_hi(2 * n - 2, l)
                        merge_hi(2 * n - 1, l)
                merge_hi(6, l)
                merge_hi(7, l)
                act.preload_act_table(ACT.Silu)
                split_hi(65, l)
                split_hi(66, l)
                for m in range(4):
                    square(l * NORMS + 3, m, y[:, m, :], tile_read, l * TILES + T_WO + m + 1 + TR0)
                split_hi(67, l)
                for m in range(4, 6):
                    square(l * NORMS + 3, m, y[:, m, :], tile_read, l * TILES + T_WO + m + 1 + TR0)
                split_hi(68, l)
                for m in range(6, 8):
                    square(l * NORMS + 3, m, y[:, m, :], tile_read, l * TILES + T_WO + m + 1 + TR0)
                pre_norm(l * NORMS + 4, g_cur[:, 4 * KD:5 * KD], l * 3 * KD + 2 * KD)
                ffn(1, l)
                with act.If(l < DEPTH - 1):
                    pre_norm(l * NORMS + NORMS, g_next, l * 3 * KD + 3 * KD)

            for n in range(3):
                act.wait_ge(final_T, n + 1)
                act.activation(out_sb[:, n % 2, n // 2 * (D // 2):(n // 2 + 1) * (D // 2)], bank[(0, 2, 1)[n]][:, :], ACT.Copy
                               ).then_inc(out_ready, 1)

        @block.vector
        def _(dve):
            dve.sem_inc(lo_done, RING)
            dve.sem_inc(tile_read, TR0)

            def split_lo(u, l, more=0):
                dve.wait_ge(hi_done, l * UNITS + u + 1 + more)
                for w, hi, lo in split_parts(u):
                    last = dve.tensor_tensor(lo, w, hi.bitcast(F32), ALU.subtract)
                last.then_inc(lo_done, 1)

            def split_lo_between(u, l, between):
                dve.wait_ge(hi_done, l * UNITS + u + 1)
                (w, hi, lo), (w2, hi2, lo2) = split_parts(u, halves=True)
                dve.tensor_tensor(lo, w, hi.bitcast(F32), ALU.subtract)
                between()
                dve.tensor_tensor(lo2, w2, hi2.bitcast(F32), ALU.subtract).then_inc(lo_done, 1)

            def tile_done(u, fin, l, mt, more_u=0, more_f=0):
                if mt == 0:
                    dve.wait_ge(first_done, l * FINISHERS + fin + 1 + more_f)
                else:
                    dve.wait_ge(unit_done, l * UNITS + u + RING + 1 + more_u)

            def layer_columns(l):
                dve.wait_ge(geo_in, 32)
                dve.wait_ge(xlo_ready, l * 4 * KD + KD)
                dve.wait_ge(h_ready, l * 3 * KD + KD)
                if_first = DEPTH * NORMS * KD
                dve.tensor_copy(g_cur[:, :], g_all[:, ds(l * (NORMS * KD), NORMS * KD)])
                dve.tensor_copy(scale_cur[:, :], g_all[:, ds(l * GROUPS + if_first, GROUPS)])
                for g in range(2):
                    dve.tensor_copy(sink_cur[:, 8 * g:8 * g + 8].rearrange("p (t s) -> p s t", s=2),
                                           sink_all[:, ds(l * HEADS + 8 * g, 8)].rearrange("p (s t) -> p s t", s=2))
                dve.tensor_copy(g_next[:, :], g_all[:, ds(l * (NORMS * KD) + NORMS * KD, KD)]).then_inc(layer_consts, 1)
                dve.wait_ge(layer_consts, l + 2)

            def mean_square(q, l):
                dve.wait_ge(ssq_done, l * NORMS + q + 2)
                dve.tensor_scalar(var[:, 0:2], small[:, S_SUM:S_SUM + 2], 1.0 / D, EPS, ALU.mult, ALU.add)
                n = T - 2 * P
                dve.tensor_scalar(var[0:n, 2:3], small[0:n, S_SUM + 2:S_SUM + 3], 1.0 / D, EPS, ALU.mult, ALU.add
                                  ).then_inc(var_ready, 1)

            def take_rms(q, l):
                dve.wait_ge(bcast_done, l * NORMS + q + 1)
                dve.tensor_copy(r[:, :], small[:, S_BC:S_BC + T]).then_inc(r_ready, 1)
                dve.wait_ge(r_ready, l * 3 + q // 2 + 1)

            def x_low(at, columns, k):
                dve.wait_ge(xhi_ready, at + k + 1)
                dve.scalar_tensor_tensor(out=x_lo[:, k, :], in0=h[:, k, :], scalar=columns[:, k:k + 1],
                                         in1=x_hi[:, k, :].bitcast(F32), op0=ALU.mult, op1=ALU.subtract
                                         ).then_inc(xlo_ready, 1)

            def boundary(n, l, at=None, columns=None):

                def normed(k):
                    dve.scalar_tensor_tensor(out=tmp[:, k % 2, 0:T], in0=y[:, k, :],
                                             scalar=g_cur[:, (2 * n + 1) * KD + k:(2 * n + 1) * KD + k + 1],
                                             in1=small[:, S_BC:S_BC + T], op0=ALU.mult, op1=ALU.mult
                                             ).then_inc(t_ready, 1)

                dve.wait_ge(bcast_done, l * NORMS + 2 * n + 2)
                normed(0)
                for k in range(KD):
                    dve.wait_ge(t_ready, l * 3 * KD + n * KD + k + 1)
                    dve.scalar_tensor_tensor(out=h[:, k, :], in0=tmp[:, k % 2, 0:T], scalar=1.0 if n == 1 else 0.5,
                                             in1=h[:, k, :], op0=ALU.mult, op1=ALU.add).then_inc(h_ready, 1)
                    if k + 1 < KD:
                        normed(k + 1)
                    if columns is not None and k >= 1:
                        x_low(at, columns, k - 1)
                if columns is not None:
                    x_low(at, columns, KD - 1)

            def take_gate(f, l, unit, mp=0):
                for j in range(2):
                    tile_done(U_FFN_IN[f] + unit, F_FFN_IN[f] + unit, l, j, mp * 2, mp * 2)
                    dve.wait_ge(silu_done, l * 2 * KF + f * KF + unit + j + 1 + mp * 2)
                    dve.tensor_tensor(gate_r[:, j, :], bank[4 * (unit // 2 % 2) + j][:, 0:T], r[:, :], ALU.mult).then_inc(tile_read, 1)

            def take_up(f, l, unit, mp=0):
                for j in range(2):
                    tile_done(U_FFN_IN[f] + unit, F_FFN_IN[f] + unit, l, j, mp * 2, mp * 2)
                    dve.wait_ge(hf_ready, l * 2 * KF + f * KF + unit - 1 + j + 1 + mp * 2)
                    dve.tensor_tensor(up_r[:, j, :], bank[2 + j][:, 0:T], r[:, :], ALU.mult).then_inc(tile_read, 1)

            def ffn(f, l):
                u0 = U_FFN_IN[f]
                split_lo_between(u0 + 3, l, lambda: mean_square(4 * f, l))
                take_rms(4 * f, l)
                take_gate(f, l, 0)
                split_lo(u0 + 4, l)
                with dve.Fori(0, 4) as i:
                    for j in range(4):
                        (take_up if j % 2 == 0 else take_gate)(f, l, 1 + j, i * 2)
                        split_lo(u0 + 5 + j, l, i * 4)
                for j in range(18, 22):
                    (take_up if j % 2 == 0 else take_gate)(f, l, j - 1, 0)
                    split_lo(u0 + j + 3, l)
                take_up(f, l, 21, 0)
                u0 = U_FFN_OUT[f]

                def take_out(i):
                    for j in range(2):
                        tile_done(u0 + 4 * i + 3, F_FFN_OUT[f] + i, l, j)
                        dve.tensor_copy(y[:, 2 * i + j, :], bank[j][:, 0:T]).then_inc(tile_read, 1)

                for i in range(3):
                    for j in range(4):
                        split_lo(u0 + 3 + 4 * i + j, l)
                    take_out(i)
                split_lo(u0 + 15, l)
                if f == 0:
                    split_lo(U_K, l)
                    split_lo(U_V, l)
                    take_out(3)
                    mean_square(1, l)
                    split_lo_between(U_Q, l, lambda: boundary(0, l, l * 4 * KD + KD, g_cur[:, 2 * KD:3 * KD]))
                else:
                    with dve.If(l < DEPTH - 1):
                        split_lo(0, l + 1)
                        split_lo(1, l + 1)
                    take_out(3)
                    mean_square(5, l)
                    with dve.If(l < DEPTH - 1):
                        split_lo_between(2, l + 1, lambda: boundary(2, l, l * 4 * KD + 4 * KD, g_next))
                    with dve.Else():
                        boundary(2, l)

            def take(u, fin, l, banks, how):
                for j in range(2):
                    tile_done(u, fin, l, j)
                    how(j, bank[banks[j]][:, 0:T]).then_inc(tile_read, 1)

            def take_q(n, l):
                take(U_Q + n, F_Q + n, l, Q_BANKS[n], lambda j, ps: dve.scalar_tensor_tensor(
                    out=qT[:, 2 * n + j, :], in0=ps, scalar=DH ** -0.5, in1=r[:, :], op0=ALU.mult, op1=ALU.mult))

            def take_pool(n, l):
                take(U_POOL + n, F_POOL + n, l, (2 - 2 * n, 3 - 2 * n), lambda j, ps: dve.tensor_tensor(
                    pool_u[:, 2 * n + j, PAD:], ps, r[:, :], ALU.mult))

            def take_gate_tile(m, l):
                tile_done(U_GATE + m // 2, F_GATE + m // 2, l, m % 2)
                dve.tensor_tensor(gates[:, m, :], bank[m % 2][:, 0:T], r[:, :], ALU.mult).then_inc(tile_read, 1)

            def step0(n, l, ins):
                ins.then_inc(s0_step, 1)
                dve.wait_ge(s0_step, l * S0_STEPS + n)

            p0 = s0[0:META, :, 0:META]

            def softmax0_shift(l):
                dve.wait_ge(s0_done, l + 1)
                dve.wait_ge(consts, l + 2)
                for side in range(2):
                    ps = (o_bank, small)[side][0:META, 0:HEADS // 2 * META].rearrange("p (c k) -> p c k", k=META)
                    last = dve.tensor_tensor(s0[0:META, side::2, 0:META], ps, causal0[:, side::2, :], ALU.add)
                step0(1, l, last)
                step0(2, l, dve.reduce_max(stats0[:, 0, :], p0, AX_X))
                step0(3, l, dve.tensor_tensor(stats0[:, 0, :], stats0[:, 0, :], sink_cur[0:META, :], ALU.max))
                step0(4, l, dve.tensor_tensor(stats0[:, 1, :], sink_cur[0:META, :], stats0[:, 0, :], ALU.subtract))
                step0(5, l, dve.tensor_tensor(p0, p0, stats0[:, 0, :].unsqueeze(2).to_broadcast([META, HEADS, META]),
                                              ALU.subtract))

            def softmax0_end(l):
                dve.wait_ge(s0_exp, l + 1)
                step0(6, l, dve.reduce_sum(stats0[:, 3, :], p0, AX_X))
                step0(7, l, dve.tensor_tensor(stats0[:, 3, :], stats0[:, 3, :], stats0[:, 2, :], ALU.add))
                step0(8, l, dve.reciprocal(stats0[:, 3, :], stats0[:, 3, :]))
                step0(9, l, dve.tensor_tensor(p0, p0, stats0[:, 3, :].unsqueeze(2).to_broadcast([META, HEADS, META]),
                                              ALU.mult))
                step0(10, l, dve.transpose(p0T[:, :, :].rearrange("p h k -> p (h k)"),
                                           s0[:, :, :].rearrange("p h k -> p (h k)")))

            def bias_and_max(i, l):
                s, st = s_buf[:, i % 3, :], stats[:, i % 3, :]
                n = l * HEADS + i + 1
                dve.wait_ge(score_done, n)
                if i >= 3:
                    dve.wait_ge(pT_done, n - 3)
                dve.scalar_tensor_tensor(out=s, in0=distance, scalar=-slopes()[head_at(i)],
                                         in1=score_bank[i % 2][:, 0:BAND], op0=ALU.mult, op1=ALU.add
                                         ).then_inc(biased, 1)
                dve.wait_ge(biased, n)
                dve.reduce_max(st[:, 0:1], s[:, 0:T], AX_X)
                dve.reduce_max(st[:, 1:2], s[:, T:BAND], AX_X).then_inc(row_max, 1)
                dve.wait_ge(row_max, n)
                dve.tensor_scalar(st[:, 2:4], st[:, 0:2], sink_cur[:, i:i + 1], -1.0, ALU.max, ALU.mult
                                  ).then_inc(neg_max, 1)

            def invert_sum(i, l):
                st = stats[:, i % 3, :]
                n = l * HEADS + i + 1
                dve.wait_ge(exp_done, n)
                dve.tensor_tensor(st[:, 4:6], st[:, 4:6], st[:, 6:8], ALU.add).then_inc(den_ready, 1)
                dve.wait_ge(den_ready, n)
                dve.reciprocal(st[:, 0:2], st[:, 4:6]).then_inc(inv_ready, 1)

            def take_o(c, l):
                dve.wait_ge(o_done, l * HEADS + 2 * c + 2)
                dve.tensor_copy(o_hi[:, c, :], o_bank[:, 0:T]).then_inc(ohi_ready, 1)
                dve.wait_ge(ohi_ready, l * KD + c + 1)
                dve.tensor_tensor(o_lo[:, c, :], o_bank[:, 0:T], o_hi[:, c, :].bitcast(F32), ALU.subtract
                                  ).then_inc(olo_ready, 1)

            def mix(g, l):
                dve.wait_ge(win_done, l * GROUPS + g + 1)
                dve.scalar_tensor_tensor(out=pool_u[:, g, PAD:], in0=win[:, g % 2, PAD:],
                                         scalar=1.0 / POOL_WINDOWS[g], in1=pool_u[:, g, PAD:],
                                         op0=ALU.mult, op1=ALU.subtract).then_inc(mixed_ready, 1)

            def take_z(g, l):
                dve.wait_ge(grp_done, l * GROUPS + g + 1)
                ps = small[:, S_BC:S_BC + T]
                dve.tensor_scalar(z_hi[:, g, :], ps, scale_cur[:, g:g + 1], None, ALU.mult).then_inc(zhi_ready, 1)
                dve.wait_ge(zhi_ready, l * GROUPS + g + 1)
                dve.scalar_tensor_tensor(out=z_lo[:, g, :], in0=ps, scalar=scale_cur[:, g:g + 1],
                                         in1=z_hi[:, g, :].bitcast(F32), op0=ALU.mult, op1=ALU.subtract
                                         ).then_inc(zlo_ready, 1)

            def gated(first_gate, n, u, fin, l):
                b = 2 * (n % 2)
                dve.wait_ge(tanh_done, l * 2 * KD + first_gate + 2 * n + 2)

                def how(j, ps):
                    g = gates[:, first_gate + 2 * n + j, :]
                    return dve.scalar_tensor_tensor(out=g, in0=g, scalar=1.0, in1=ps, op0=ALU.add, op1=ALU.mult)

                take(u, fin, l, (b, b + 1), how)

            def merge_lo(m, l):
                dve.wait_ge(xhi_ready, l * 4 * KD + 2 * KD + m + 1)
                dve.scalar_tensor_tensor(out=x_lo[:, m, :], in0=gates[:, m, :], scalar=0.5,
                                         in1=x_hi[:, m, :].bitcast(F32), op0=ALU.mult, op1=ALU.subtract
                                         ).then_inc(xlo_ready, 1)

            dve.wait_ge(first_T, 1)
            dve.tensor_copy(g_all[:, :], small[:, 0:n_rows]).then_inc(rows_read, 1)
            for k in range(KD):
                dve.wait_ge(first_T, k + 2)
                dve.tensor_copy(h[:, k, :], bank[k % 4][:, 0:T]).then_inc(h_ready, 1)
            dve.wait_ge(rows_read, 1)
            dve.tensor_copy(g_next[:, :], g_all[:, 0:KD]).then_inc(layer_consts, 1)
            dve.wait_ge(layer_consts, 1)
            split_lo(0, 0)
            split_lo(1, 0)
            for k in range(KD):
                x_low(0, g_next, k)
            split_lo(2, 0)

            with dve.Fori(0, DEPTH) as l:
                layer_columns(l)
                ffn(0, l)
                split_lo_between(41, l, lambda: mean_square(2, l))
                take_rms(2, l)
                take(U_K, F_KV, l, (0, 1), lambda j, ps: dve.tensor_tensor(kT[:, j, :], ps, r[:, :], ALU.mult))
                take(U_V, F_KV + 1, l, (2, 3), lambda j, ps: dve.tensor_tensor(vT[:, j, :], ps, r[:, :], ALU.mult))
                split_lo(42, l)
                split_lo(43, l)
                for n in range(4):
                    take_q(n, l)
                    split_lo(44 + n, l)
                take_pool(0, l)
                softmax0_shift(l)
                split_lo(48, l)
                take_pool(1, l)
                for i in range(HEADS + 4):
                    if i >= 5 and i % 2 == 1:
                        take_o((i - 5) // 2, l)
                    if 1 <= i <= HEADS:
                        take_gate_tile(i - 1, l)
                        invert_sum(i - 1, l)
                    if i - 1 in GROUP_STEPS:
                        take_z(GROUP_STEPS.index(i - 1), l)
                    if i % 2 == 1 and i < HEADS:
                        split_lo(49 + i // 2, l)
                    if i < HEADS:
                        bias_and_max(i, l)
                    if i == 0:
                        softmax0_end(l)
                    if HEADS <= i < HEADS + 3:
                        split_lo(57 + i - HEADS, l)
                        if i > HEADS:
                            n = i - HEADS - 1
                            gated(0, n, U_PP + n, F_PP + n, l)
                    if i in MIX_STEPS:
                        mix(MIX_STEPS.index(i), l)
                gated(0, 2, U_PP + 2, F_PP + 2, l)
                split_lo(60, l)
                gated(0, 3, U_PP + 3, F_PP + 3, l)
                for n in range(4):
                    split_lo(61 + n, l)
                    gated(KD, n, U_AP + n, F_AP + n, l)
                    if n >= 1:
                        merge_lo(2 * n - 2, l)
                        merge_lo(2 * n - 1, l)
                merge_lo(6, l)
                merge_lo(7, l)
                split_lo(65, l)

                def take_y(n):
                    b = 2 * (n % 2)
                    take(U_WO + n, F_WO + n, l, (b, b + 1), lambda j, ps: dve.tensor_copy(y[:, 2 * n + j, :], ps))

                take_y(0)
                take_y(1)
                split_lo(66, l)
                split_lo(67, l)
                take_y(2)
                take_y(3)
                mean_square(3, l)
                split_lo_between(68, l, lambda: boundary(1, l, l * 4 * KD + 3 * KD, g_cur[:, 4 * KD:5 * KD]))
                ffn(1, l)

            dve.wait_ge(final_T, 4)
            dve.tensor_copy(out_sb[:, 1, D // 2:D], bank[3][:, :]).then_inc(out_late, 1)

        @block.gpsimd
        def _(pool):
            pool.sem_inc(hf_ready, 2)
            pool.memset(ident[:, :], 0.0).then_inc(win_step, 1)
            pool.memset(half[:, :], -0.5)
            pool.memset(var[:, :], 1.0)
            pool.memset(ones[:, :], 1.0)
            pool.wait_ge(win_step, 1)
            pool.affine_select(out=ident[:, :], in_=ident[:, :], compare_op=ALU.not_equal, fill=1.0, base=0,
                               pattern=[[-1, P]], channel_multiplier=1).then_inc(consts, 1)

            def add_squares(q, l):
                for m in range(1, KD - 2):
                    pool.wait_ge(sq_done, (l * NORMS + q) * KD + m + 1)
                    if m == 1:
                        pool.wait_ge(ssq_done, l * NORMS + q + 1)
                        pool.tensor_tensor(acc[:, :], sq[:, 0, :], sq[:, 1, :], ALU.add).then_inc(acc_done, 1)
                    else:
                        pool.wait_ge(acc_done, (l * NORMS + q) * (KD - 3) + m - 1)
                        pool.tensor_tensor(acc[:, :], acc[:, :], sq[:, m % 2, :], ALU.add).then_inc(acc_done, 1)

            def inverse_rms(q, l):
                pool.wait_ge(var_ready, l * NORMS + q + 1)
                pool.tensor_tensor(rt[:, 0:3], var[:, 0:3], half[:, 0:3], ALU.pow).then_inc(rt_ready, 1)

            def ffn(f, l):
                add_squares(4 * f, l)
                inverse_rms(4 * f, l)
                with pool.Fori(0, KF // 2) as i:
                    for j in range(2):
                        n = l * 2 * KF + f * KF + i * 2 + j
                        pool.wait_ge(silu_done, n + 3)
                        pool.wait_ge(tile_read, l * TILES + T_FFN_IN[f] + i * 4 + 3 + j + TR0)
                        pool.tensor_tensor(hid_hi[:, ds(i * 2 + j, 1), :].rearrange("p o t -> p (o t)"), silu[:, j, :],
                                           up_r[:, j, :], ALU.mult).then_inc(hid_hi_ready, 1)
                        pool.tensor_tensor(hid_f[:, j, :], silu[:, j, :], up_r[:, j, :], ALU.mult).then_inc(hf_ready, 1)
                        pool.wait_ge(hid_hi_ready, n + 1)
                        pool.wait_ge(hf_ready, n + 3)
                        pool.tensor_tensor(hid_lo[:, ds(i * 2 + j, 1), :].rearrange("p o t -> p (o t)"), hid_f[:, j, :],
                                           hid_hi[:, ds(i * 2 + j, 1), :].rearrange("p o t -> p (o t)").bitcast(F32),
                                           ALU.subtract).then_inc(hid_ready, 1)
                add_squares(4 * f + 1, l)
                inverse_rms(4 * f + 1, l)

            def window(g, l):
                done = sum(n + 2 for n in range(g))
                src, at = pool_u[:, g, :], 0
                for d in range(g + 1):
                    lag = 1 << d
                    dst = win[:, (2 * g - d) % 2, :]
                    a = at + lag
                    pool.tensor_tensor(dst[:, a:], src[:, a:], src[:, a - lag:PAD + T - lag], ALU.add
                                       ).then_inc(win_step, 1)
                    src, at = dst, a
                    pool.wait_ge(win_step, l * WIN_STEPS + done + d + 2)
                pool.tensor_tensor(src[:, PAD:2 * PAD], src[:, PAD:2 * PAD], ramp[:, g, :], ALU.mult
                                   ).then_inc(win_step, 1)
                pool.wait_ge(win_step, l * WIN_STEPS + done + g + 3)
                pool.sem_inc(win_done, 1)

            def normalise(i, l):
                s, st = s_buf[:, i % 3, :], stats[:, i % 3, :]
                pool.wait_ge(inv_ready, l * HEADS + i + 1)
                pool.tensor_tensor(s[:, 0:T], s[:, 0:T], st[:, 0:1].to_broadcast([P, T]), ALU.mult)
                pool.tensor_tensor(s[:, T:BAND], s[:, T:BAND], st[:, 1:2].to_broadcast([P, BAND - T]), ALU.mult
                                   ).then_inc(p_ready, 1)

            with pool.Fori(0, DEPTH) as l:
                ffn(0, l)
                add_squares(2, l)
                inverse_rms(2, l)
                pool.memset(pool_u[:, :, 0:PAD], 0.0)
                pool.memset(s0[:, :, :], 0.0).then_inc(consts, 1)
                pool.wait_ge(consts, l + 2)
                for i in range(HEADS + 1):
                    if i in WINDOW_STEPS:
                        g = WINDOW_STEPS.index(i)
                        pool.wait_ge(tile_read, l * TILES + T_POOL + g + 1 + TR0)
                        if g >= 1:
                            pool.wait_ge(mixed_ready, l * GROUPS + g)
                        window(g, l)
                    if i >= 1:
                        normalise(i - 1, l)
                for m in range(KD):
                    pool.wait_ge(tile_read, l * TILES + T_AP + m + 1 + TR0)
                    pool.tensor_tensor(gates[:, m, :], gates[:, m, :], gates[:, KD + m, :], ALU.add
                                       ).then_inc(merged, 1)
                add_squares(3, l)
                inverse_rms(3, l)
                ffn(1, l)


Q_BANKS = ((4, 5), (0, 1), (2, 3), (0, 1))
WARM_RMS, WARM_X = 8, 10
WINDOW_STEPS = (0, 2, 4, 6)
MIX_STEPS = (1, 3, 5, 7)
GROUP_STEPS = (3, 5, 7, 9)
S0_STEPS, S0_SHIFTED = 10, 5


def geometry_table():
    keys = np.arange(T)
    parts = []
    for first, n_keys in ((META + P, T), (META, META + P)):
        d = (first + np.arange(P))[:, None] - keys[None, :n_keys]
        parts.append(np.where(keys[None, :n_keys] < META, 0.0, np.where((d >= 0) & (d < WINDOW), d, FAR)))
    k = np.arange(META)
    mask = np.where(k[None, :] <= (np.arange(P)[:, None] % META), 0.0, -1e30)
    parts.append(np.tile(mask, (1, HEADS)))
    t = np.arange(PAD) + 1
    parts.append(np.tile(np.concatenate([w / np.minimum(t, w) for w in POOL_WINDOWS])[None], (P, 1)))
    return np.concatenate(parts, axis=1).astype(np.float32)


_INS = ["x", "meta_tokens", "norm_g", "ffn_w_in", "ffn_w_out", "w_in", "pool_w_grp", "pool_scale",
        "w_pool_proj", "sinks", "w_attn_proj", "w_o"]


def kernel(**inputs):
    import concourse.bacc as bacc
    from concourse.bass_utils import run_bass_kernel_spmd

    nc = bacc.Bacc("TRN2", target_bir_lowering=False, num_devices=1)
    arrays, args = {}, []
    for name in _INS + ["geometry"]:
        a = geometry_table() if name == "geometry" else np.ascontiguousarray(inputs[name])
        arrays[f"in_{name}"] = a
        args.append(nc.dram_tensor(f"in_{name}", a.shape, F32, kind="ExternalInput").ap())
    args.append(nc.dram_tensor("out_h", (1, SEQ, D), F32, kind="ExternalOutput").ap())
    trunk(nc, *args)
    result = run_bass_kernel_spmd(nc, [arrays], core_ids=[0])
    return result.results[0]["out_h"]
```

```python
from contextlib import ExitStack

import numpy as np
import concourse.bass as bass
from concourse import mybir

F32 = mybir.dt.float32
F32R = mybir.dt.float32r
ALU = mybir.AluOpType
ACT = mybir.ActivationFunctionType
AX_X = mybir.AxisListType.X
ds = bass.ds

P = 128
D = 1024
SEQ = 256
META = 16
T = META + SEQ
DEPTH = 2
HEADS, KV_HEADS, DH = 16, 4, 64
WINDOW = 128
POOL_WINDOWS = (2, 4, 8, 16)
GROUPS = len(POOL_WINDOWS)
POOL_DIM = GROUPS * P
Q_DIM = HEADS * DH
KV_DIM = KV_HEADS * DH
FF = ((8 * D // 3 + 127) // 128) * 128
EPS = 1e-6
KD = D // P
KF = FF // P
UW = 2 * P
RING = 4
OUT_K = (6, 5, 6, 5)
OUT_K0 = (0, 6, 11, 17)
B1, B2 = slice(META, META + P), slice(META + P, T)
BAND = T + META + P
FAR = 1e33
PAD = POOL_WINDOWS[-1]

U_FFN_IN = (0, 66)
U_FFN_OUT = (22, 88)
U_K, U_V, U_Q, U_POOL, U_GATE, U_PP, U_AP, U_WO = 38, 39, 40, 44, 46, 54, 58, 62
UNITS = 104
N_IN, N_OUT = FF * 2 // UW, 16
assert N_IN == 22 and sum(OUT_K) == KF and UNITS % RING == 0
T_FFN_IN, T_FFN_OUT = (0, 108), (44, 152)
T_KV, T_Q, T_POOL, T_GATE, T_PP, T_AP, T_WO = 52, 56, 64, 68, 84, 92, 100
TILES = 160
F_FFN_IN, F_FFN_OUT = (0, 54), (22, 76)
F_KV, F_Q, F_POOL, F_GATE, F_PP, F_AP, F_WO = 26, 28, 32, 34, 42, 46, 50
FINISHERS = 80
FFN_LAG = 8
TR0 = FFN_LAG - 4
NORMS = 6


def slopes():
    return [2.0 ** (-8.0 * (h + 1) / HEADS) for h in range(HEADS)]


def head_at(i):
    tile, side = divmod(i, 2)
    group, t = divmod(tile, 4)
    return 8 * group + 4 * side + t


def kv_at(i):
    tile, side = divmod(i, 2)
    return 2 * (tile // 4) + side


def unit_k(u):
    for first in U_FFN_OUT:
        if first <= u < first + N_OUT:
            return OUT_K[(u - first) % 4]
    return GROUPS if U_PP <= u < U_AP else KD


def unit_dmas(u):
    return 2 if U_Q <= u < U_POOL else 4 if U_AP <= u < U_WO else 1


SLOT_DMAS = [sum(unit_dmas(u) for u in range(s, UNITS, RING)) for s in range(RING)]


def landed_at(u, layer, more=0):
    upto = sum(unit_dmas(v) for v in range(u % RING, u + 1, RING))
    return (layer * SLOT_DMAS[u % RING] + upto + more) * 16


def trunk(nc, x, meta_tokens, norm_g, ffn_w_in, ffn_w_out, w_in, pool_w_grp, pool_scale, w_pool_proj,
          sinks, w_attn_proj, w_o, geometry, out):
    with ExitStack() as ctx:
        def sb(name, shape, dt=F32):
            return ctx.enter_context(nc.sbuf_tensor(name, shape, dt))

        def sem(name):
            return ctx.enter_context(nc.semaphore(name))

        raw = sb("raw", [P, RING, KD * UW])
        w_hi = sb("w_hi", [P, RING, KD * UW], F32R)
        w_lo = sb("w_lo", [P, RING, KD * UW], F32R)
        h = sb("h", [P, KD, T])
        x_hi = sb("x_hi", [P, KD, T], F32R)
        x_lo = sb("x_lo", [P, KD, T], F32R)
        y = sb("y", [P, KD, T])
        sq = sb("sq", [P, 2, T])
        acc = sb("acc", [P, T])
        r = sb("r", [P, T])
        tmp = sb("tmp", [P, 2, PAD + T])
        var = sb("var", [P, 4])
        rt = sb("rt", [P, 4])
        half = sb("half", [P, 4])
        ident = sb("ident", [P, P])
        ones = sb("ones", [P, 1])
        g_all = sb("g_all", [P, DEPTH * NORMS * KD + DEPTH * GROUPS])
        g_cur = sb("g_cur", [P, NORMS * KD])
        half_g = sb("half_g", [P, KD])
        g_next = sb("g_next", [P, KD])
        scale_cur = sb("scale_cur", [P, GROUPS])
        sink_all = sb("sink_all", [P, DEPTH * HEADS])
        sink_cur = sb("sink_cur", [P, HEADS])
        geo = sb("geo", [P, BAND + META + GROUPS * PAD])
        distance = geo[:, 0:BAND]
        causal0 = geo[0:META, BAND:BAND + META]
        ramp = geo[:, BAND + META:].rearrange("p (g t) -> p g t", g=GROUPS)

        def sizes(items):
            return sum(-(-int(np.prod(s[1:])) * 4 // 32) * 32 for _, s, _ in items)

        ffn_items = [("hid_hi", [P, KF, T], F32R), ("hid_lo", [P, KF, T], F32R), ("gate_r", [P, 2, T], F32),
                     ("silu", [P, 2, T], F32), ("up_r", [P, 2, T], F32), ("hid_f", [P, 2, T], F32)]
        mix_items = [("kT", [P, 2, T], F32), ("v_tok", [P, 2, KV_DIM], F32), ("v_meta", [META, KV_DIM], F32),
                     ("v_pair", [4 * META, 2, P], F32),
                     ("gates", [P, 2 * KD, T], F32), ("pool_u", [P, GROUPS, PAD + T], F32),
                     ("z_hi", [P, GROUPS, T], F32R),
                     ("z_lo", [P, GROUPS, T], F32R), ("o_hi", [P, KD, T], F32R), ("o_lo", [P, KD, T], F32R),
                     ("s", [P, 3, BAND], F32), ("pT", [P, 2, 3 * P], F32), ("pT_meta", [4 * META, 2, 2 * P], F32),
                     ("s0", [32, HEADS, 32], F32), ("stats0", [META, 4, HEADS], F32),
                     ("stats", [P, 3, 8], F32), ("w_grp", [P, GROUPS, P], F32)]
        arena_bytes = max(sizes(ffn_items), sizes(mix_items))
        arena = sb("arena", [P, arena_bytes // 4])
        base = nc.sbuf_base - arena_bytes

        def place(items):
            at, placed = base, []
            for name, shape, dt in items:
                placed.append(nc.alloc_sbuf_tensor_at(name, shape, dt, offset=at))
                at += sizes([(name, shape, dt)])
            return placed

        hid_hi, hid_lo, gate_r, silu, up_r, hid_f = place(ffn_items)
        (kT, v_tok, v_meta, v_pair, gates, pool_u, z_hi, z_lo, o_hi, o_lo, s_buf, pT, pT_meta, s0, stats0,
         stats, w_grp) = place(mix_items)
        win = tmp
        vT_pair = tmp[:, :, 0:P]
        p_meta = acc
        p0T = sq[0:32].rearrange("p a t -> p (a t)")[:, 0:HEADS * 32].rearrange("p (h k) -> p h k", h=HEADS)
        qT = y
        vT = gates[:, 2 * KD - 2:2 * KD, :]
        first_x = gates[:, 0:8, :].rearrange("p a t -> p (a t)")[:, 0:2 * D].rearrange("p (b d) -> p b d", b=2)
        first_meta = gates[0:META, 8:12, :].rearrange("p a t -> p (a t)")[:, 0:D]
        n_rows = DEPTH * NORMS * KD + DEPTH * GROUPS
        first_rows = gates[0:n_rows, 12, 0:P]
        out_sb = gates[:, 0:8, :].rearrange("p a t -> p (a t)")[:, 0:2 * D].rearrange("p (b d) -> p b d", b=2)

        bank = [ctx.enter_context(nc.psum_tensor(f"bank{b}", [P, 512], F32)) for b in range(8)]
        score_bank = (bank[2], bank[3])
        pT_bank, pTm_bank, o_bank, small = bank[4], bank[5], bank[6], bank[7]
        warm = o_bank
        S_SUM, S_BC = 0, 128

        inputs_in = sem("inputs_in")
        second_half_in = sem("second_half_in")
        geo_in = sem("geo_in")
        raw_landed = [sem(f"raw_landed{s}") for s in range(RING)]
        w_grp_in = sem("w_grp_in")
        out_stored = sem("out_stored")
        consts = sem("consts")
        hi_done = sem("hi_done")
        lo_done = sem("lo_done")
        unit_done = sem("unit_done")
        first_done = sem("first_done")
        tile_read = sem("tile_read")
        layer_consts = sem("layer_consts")
        first_T = sem("first_T")
        rows_read = sem("rows_read")
        h_ready = sem("h_ready")
        even_h_ready = sem("even_h_ready")
        odd_h_ready = sem("odd_h_ready")
        t_ready = sem("t_ready")
        xhi_ready = sem("xhi_ready")
        xlo_ready = sem("xlo_ready")
        sq_done = sem("sq_done")
        acc_done = sem("acc_done")
        ssq_done = sem("ssq_done")
        var_ready = sem("var_ready")
        rt_ready = sem("rt_ready")
        bcast_done = sem("bcast_done")
        r_ready = sem("r_ready")
        silu_done = sem("silu_done")
        hf_ready = sem("hf_ready")
        hid_hi_ready = sem("hid_hi_ready")
        hid_ready = sem("hid_ready")
        v_spread = sem("v_spread")
        v_turned = sem("v_turned")
        v_ready = sem("v_ready")
        s0_done = sem("s0_done")
        s0_step = sem("s0_step")
        s0_exp = sem("s0_exp")
        score_done = sem("score_done")
        biased = sem("biased")
        row_max = sem("row_max")
        neg_max = sem("neg_max")
        exp_done = sem("exp_done")
        den_ready = sem("den_ready")
        inv_ready = sem("inv_ready")
        p_ready = sem("p_ready")
        pT_done = sem("pT_done")
        pT_ready = sem("pT_ready")
        o_done = sem("o_done")
        ohi_ready = sem("ohi_ready")
        olo_ready = sem("olo_ready")
        tanh_done = sem("tanh_done")
        win_step = sem("win_step")
        win_done = sem("win_done")
        mixed_ready = sem("mixed_ready")
        grp_done = sem("grp_done")
        zhi_ready = sem("zhi_ready")
        zlo_ready = sem("zlo_ready")
        merged = sem("merged")
        final_T = sem("final_T")
        out_ready = sem("out_ready")
        out_late = sem("out_late")

        def split_parts(u, halves=False):
            s, n = u % RING, unit_k(u) * UW
            if not U_Q <= u < U_POOL:
                cuts = (0, n // 2, n) if halves else (0, n)
                return [(raw[:, s, a:b], w_hi[:, s, a:b], w_lo[:, s, a:b]) for a, b in zip(cuts, cuts[1:])]
            from_raw = raw[:, s, :].rearrange("p (k s t c) -> p t k s c", s=2, t=2, c=DH)
            to_hi, to_lo = (w[:, s, :].rearrange("p (k t s c) -> p t k s c", s=2, t=2, c=DH) for w in (w_hi, w_lo))
            return [(from_raw[:, t], to_hi[:, t], to_lo[:, t]) for t in range(2)]

        block = ctx.enter_context(nc.Block())

        WIN_STEPS = sum(g + 2 for g in range(GROUPS))

        @block.sync
        def _(sp):
            sp.dma_start(first_x[:, :, 0:D // 2], x[0, :, 0:D // 2].rearrange("(b p) d -> p b d", b=2)
                         ).then_inc(inputs_in, 16)
            sp.dma_start(first_meta, meta_tokens).then_inc(inputs_in, 16)
            sp.dma_start(first_rows[0:DEPTH * NORMS * KD, :], norm_g.rearrange("l n (k p) -> (l n k) p", p=P)
                         ).then_inc(inputs_in, 16)
            sp.dma_start(first_rows[DEPTH * NORMS * KD:n_rows, :], pool_scale.rearrange("l (g p) -> (l g) p", p=P)
                         ).then_inc(inputs_in, 16)
            sp.dma_start(first_x[:, :, D // 2:D], x[0, :, D // 2:D].rearrange("(b p) d -> p b d", b=2)
                         ).then_inc(second_half_in, 16)

            def slot_free(u, l, more=0):
                sp.wait_ge(lo_done, l * UNITS + u + 1 + more)

            def load(u, src, dst=None):
                s = u % RING
                to = raw[:, s, 0:unit_k(u) * UW].rearrange("p (k c) -> p k c", c=UW) if dst is None else dst
                sp.dma_start(to, src).then_inc(raw_landed[s], 16)

            def ffn_loads(l, f):
                w1 = ffn_w_in[ds(l, 1), f].rearrange("o (k p) n -> p (o k) n", p=P)
                w2 = ffn_w_out[ds(l, 1), f].rearrange("o (k p) n -> p (o k) n", p=P)
                u0 = U_FFN_IN[f]
                for j in range(2):
                    slot_free(u0 + j, l)
                    load(u0 + j, w1[:, :, j * FF:j * FF + UW])
                with sp.Fori(0, N_IN - 5, 4) as i:
                    for j in range(4):
                        slot_free(u0 + 2 + j, l, i)
                        load(u0 + 2 + j, w1[:, :, ds(i * (UW // 2) + (UW * (1 + j // 2) + j % 2 * FF), UW)])
                u0 = U_FFN_OUT[f]
                with sp.Fori(0, N_OUT - 3, 4) as i:
                    for j in range(4):
                        slot_free(u0 + j, l, i)
                        load(u0 + j, w2[:, OUT_K0[j]:OUT_K0[j] + OUT_K[j], ds(i * (UW // 4), UW)])

            with sp.Fori(0, DEPTH) as l:
                ffn_loads(l, 0)
                w = w_in[ds(l, 1)].rearrange("o (k p) n -> p (o k) n", p=P)
                q0, k0 = POOL_DIM, POOL_DIM + Q_DIM
                v0, g0 = k0 + KV_DIM, k0 + 2 * KV_DIM
                for u in range(U_K, U_PP):
                    slot_free(u, l)
                    if u == U_POOL:
                        sp.wait_ge(unit_done, l * UNITS + U_K + RING)
                        sp.dma_start(w_grp[:, :, :], pool_w_grp[ds(l, 1)].rearrange("o g c d -> c (o g) d")
                                     ).then_inc(w_grp_in, 16)
                    if U_Q <= u < U_POOL:
                        c = q0 + (8 * ((u - U_Q) // 2) + 2 * ((u - U_Q) % 2)) * DH
                        to = raw[:, u % RING, :].rearrange("p (k s c) -> p k s c", s=2, c=P)
                        for side in range(2):
                            load(u, w[:, :, c + side * 4 * DH:c + side * 4 * DH + P], to[:, :, side, :])
                    else:
                        c = (k0 if u == U_K else v0 if u == U_V else (u - U_POOL) * UW if u < U_GATE
                             else g0 + (u - U_GATE) * UW)
                        load(u, w[:, :, c:c + UW])
                wp = w_pool_proj[ds(l, 1)].rearrange("o (k p) n -> p (o k) n", p=P)
                for m in range(4):
                    slot_free(U_PP + m, l)
                    load(U_PP + m, wp[:, :, m * UW:(m + 1) * UW])
                wa = w_attn_proj[ds(l, 1)].rearrange("o (g s t f) n -> g s f (o t) n", g=2, s=2, t=4)
                for m in range(4):
                    u = U_AP + m
                    slot_free(u, l)
                    to = raw[:, u % RING, :].rearrange("p (g t c) -> p g t c", g=2, t=4)
                    for g in range(2):
                        for side in range(2):
                            load(u, wa[g, side, :, :, m * UW:(m + 1) * UW], to[side * DH:(side + 1) * DH, g])
                wo = w_o[ds(l, 1)].rearrange("o (k p) n -> p (o k) n", p=P)
                for m in range(4):
                    slot_free(U_WO + m, l)
                    load(U_WO + m, wo[:, :, m * UW:(m + 1) * UW])
                ffn_loads(l, 1)

            for half_d in range(2):
                for b in range(2):
                    if half_d == 1 and b == 1:
                        sp.wait_ge(out_late, 1)
                    else:
                        sp.wait_ge(out_ready, 2 * half_d + b + 1)
                    c = slice(half_d * (D // 2), (half_d + 1) * (D // 2))
                    sp.dma_start(out[0, b * P:(b + 1) * P, c], out_sb[:, b, c]).then_inc(out_stored, 16)
            sp.wait_ge(out_stored, 16 * 4)

        @block.tensor
        def _(pe):
            pe.sem_inc(unit_done, RING)
            pe.sem_inc(ssq_done, 1)

            def weights(u, k, mt):
                s = u % RING
                return [w[:, s, k * UW + mt * P:k * UW + (mt + 1) * P] for w in (w_hi, w_lo)]

            def products(ps, w, a_hi, a_lo, start, stop, t0):
                pe.matmul(ps[:, t0:T], w[0], a_hi[:, t0:T], start=start, stop=False)
                pe.matmul(ps[:, t0:T], w[0], a_lo[:, t0:T], start=False, stop=False)
                return pe.matmul(ps[:, t0:T], w[1], a_hi[:, t0:T], start=False, stop=stop)

            def unit_split(u, l, more=0):
                pe.wait_ge(lo_done, l * UNITS + u + RING + 1 + more)

            def tile_free(t, l, lag, more=0):
                pe.wait_ge(tile_read, l * TILES + t - lag + 1 + TR0 + more)

            def deep_pair(u, l, a_hi, a_lo, operand_ready, extra=None, t=None, t0=0):
                unit_split(u, l)
                unit_split(u + 1, l)
                for k in range(KD):
                    operand_ready(k)
                    for c in range(4):
                        if k == 0 and t is not None:
                            tile_free(t + c, l, 4)
                        if k == KD - 1 and c == 0 and extra is not None:
                            extra()
                        last = products(bank[c], weights(u + c // 2, k, c % 2), a_hi[:, k, :], a_lo[:, k, :],
                                        k == 0, k == KD - 1, t0)
                        if k == KD - 1:
                            last.then_inc(first_done if c % 2 == 0 else unit_done, 1)

            def pair_in_turn(u, l, a_hi, a_lo, operand_ready, extra):
                for c in range(2):
                    unit_split(u + c, l)
                    for k in range(KD):
                        if c == 0:
                            operand_ready(k)
                        elif k == KD - 1:
                            extra()
                        for mt in range(2):
                            last = products(bank[2 * c + mt], weights(u + c, k, mt), a_hi[:, k, :], a_lo[:, k, :],
                                            k == 0, k == KD - 1, 0)
                            if k == KD - 1:
                                last.then_inc(first_done if mt == 0 else unit_done, 1)

            def unit_tile(u, l, mt, b, nk, a_hi, a_lo, t0=0):
                for k in range(nk):
                    last = products(bank[b], weights(u, k, mt), a_hi[:, k, :], a_lo[:, k, :], k == 0, k == nk - 1, t0)
                last.then_inc(first_done if mt == 0 else unit_done, 1)

            def unit(u, l, t, banks, lag, nk, a_hi, a_lo, more=0, more_t=0, t0=0):
                unit_split(u, l, more)
                for mt in range(2):
                    tile_free(t + mt, l, lag, more_t)
                    unit_tile(u, l, mt, banks[mt], nk, a_hi, a_lo, t0)

            def sum_squares(q, l):
                n = l * NORMS + q
                if q % 2 == 1:
                    pe.wait_ge(r_ready, l * 3 + q // 2 + 1)
                for part in range(3):
                    if part == 0:
                        pe.wait_ge(acc_done, (n + 1) * (KD - 3))
                    else:
                        pe.wait_ge(sq_done, (n + 1) * KD + part - 2)
                    src = acc[:, :] if part == 0 else sq[:, part - 1, :]
                    for b in range(3):
                        m = min(P, T - b * P)
                        last = pe.matmul(small[0:m, S_SUM + b:S_SUM + b + 1], src[:, b * P:b * P + m], ones[:, 0:1],
                                         start=(part == 0 and b == 0), stop=(part == 2), skip_group_check=True)
                last.then_inc(ssq_done, 1)

            def keep_warm(n):
                for _ in range(n):
                    pe.matmul(warm[:, 0:P], ident[:, :], ident[:, :], start=True, stop=True)

            def spread_rms(q, l):
                pe.wait_ge(rt_ready, l * NORMS + q + 1)
                for b in range(3):
                    n = min(P, T - b * P)
                    last = pe.matmul(small[:, S_BC + b * P:S_BC + b * P + n], rt[0:n, b:b + 1].to_broadcast([n, P]),
                                     ident[0:n, 0:n], start=True, stop=True)
                last.then_inc(bcast_done, 1)

            def x_tile(n, l):
                pe.wait_ge(xlo_ready, l * 4 * KD + n + 1)

            def ffn(f, l, t0=0):
                u0, tile0 = U_FFN_IN[f], T_FFN_IN[f]
                first_pair = (u0, l, x_hi, x_lo, lambda k: x_tile((0, 3 * KD)[f] + k, l), lambda: sum_squares(4 * f, l))
                if f == 0:
                    with pe.If(l < 1):
                        pair_in_turn(*first_pair)
                    with pe.Else():
                        deep_pair(*first_pair)
                else:
                    deep_pair(*first_pair, t0=t0)
                spread_rms(4 * f, l)
                with pe.Fori(0, (N_IN - 2) // 4) as i:
                    for j in range(4):
                        banks, lag = (((4, 5), FFN_LAG), ((2, 3), 4), ((0, 1), FFN_LAG), ((2, 3), 4))[j]
                        unit(u0 + 2 + j, l, tile0 + 4 + 2 * j, banks, lag, KD, x_hi, x_lo, i * 4, i * 8, t0)
                u0, tile0 = U_FFN_OUT[f], T_FFN_OUT[f]
                with pe.Fori(0, N_OUT // 8) as i:
                    for u in range(8):
                        pair, j = divmod(u, 4)
                        unit_split(u0 + u, l, i * 8)
                        pe.wait_ge(hid_ready, l * 2 * KF + f * KF + OUT_K0[j] + OUT_K[j])
                        for mt in range(2):
                            if j == 0:
                                tile_free(tile0 + 2 * pair + mt, l, 4, i * 4)
                            for k in range(OUT_K[j]):
                                kk = OUT_K0[j] + k
                                last = products(bank[2 * pair + mt], weights(u0 + u, k, mt), hid_hi[:, kk, :],
                                                hid_lo[:, kk, :], kk == 0, kk == KF - 1, t0)
                            if mt == 0 and j == 3:
                                last.then_inc(first_done, 1)
                        last.then_inc(unit_done, 1)
                sum_squares(4 * f + 1, l)
                keep_warm(WARM_RMS)
                spread_rms(4 * f + 1, l)
                keep_warm(WARM_X)

            def turn_v(l):
                for j in range(2):
                    for b, blk in enumerate((B1, B2)):
                        pe.transpose(pT_bank[:, b * KV_DIM + j * P:b * KV_DIM + (j + 1) * P], vT[:, j, blk], ident[:, :])
                for j in range(2):
                    pe.transpose(pTm_bank[:, j * P:(j + 1) * P], vT[:, j, 0:P], ident[:, :])
                pe.wait_ge(v_spread, l + 1)
                for j in range(2):
                    last = pe.transpose(pTm_bank[:, KV_DIM + j * P:KV_DIM + (j + 1) * P], vT_pair[:, j, :], ident[:, :])
                last.then_inc(v_turned, 1)

            def rows(i):
                return slice((i % 2) * DH, (i % 2) * DH + DH)

            def scores0(l):
                for i in range(HEADS):
                    last = pe.matmul((o_bank, small)[i % 2][0:META, i // 2 * META:(i // 2 + 1) * META], qT[rows(i), i // 2, 0:META],
                                     kT[rows(i), i // 8, 0:META], start=True, stop=True)
                last.then_inc(s0_done, 1)

            def scores(i, l):
                if i >= 2:
                    pe.wait_ge(biased, l * HEADS + i - 1)
                sc = score_bank[i % 2]
                pe.matmul(sc[:, 0:T], qT[rows(i), i // 2, B2], kT[rows(i), i // 8, 0:T], start=True, stop=True)
                pe.matmul(sc[:, T:BAND], qT[rows(i), i // 2, B1], kT[rows(i), i // 8, 0:META + P], start=True,
                          stop=True).then_inc(score_done, 1)

            def turn_p(i, l):
                pe.wait_ge(p_ready, l * HEADS + i + 1)
                if i >= 1:
                    pe.wait_ge(pT_ready, l * HEADS + i)
                s = s_buf[:, i % 3, :]
                pe.transpose(pT_bank[:, 0:P], s[:, T + META:BAND], ident[:, :])
                pe.transpose(pT_bank[:, P:2 * P], s[:, META:META + P], ident[:, :])
                last = pe.transpose(pT_bank[:, 2 * P:3 * P], s[:, META + P:T], ident[:, :])
                if i % 2 == 1:
                    c = i // 2 % 2 * P
                    last = pe.transpose(pTm_bank[:, 0:P], p_meta[:, c:c + P], ident[:, :])
                last.then_inc(pT_done, 1)

            def attend(i, l):
                pe.wait_ge(pT_ready, l * HEADS + i + 1)
                if i == 0:
                    pe.wait_ge(v_ready, 2 * l + 2)
                    pe.wait_ge(s0_step, (l + 1) * S0_STEPS)
                if i % 2 == 0 and i >= 2:
                    pe.wait_ge(olo_ready, l * KD + i // 2)
                o = o_bank[rows(i), :]
                c = slice(kv_at(i) * DH, (kv_at(i) + 1) * DH)
                pe.matmul(o[:, 0:META], v_meta[0:META, c], p0T[0:META, i, 0:META], start=True, stop=False,
                          skip_group_check=True)
                pe.matmul(o[:, META:T], v_tok[:, 0, c], pT[:, i % 2, 0:2 * P], start=False, stop=False,
                          skip_group_check=True)
                last = pe.matmul(o[:, META + P:T], v_tok[:, 1, c], pT[:, i % 2, 2 * P:3 * P], start=False,
                                 stop=i % 2 == 0, skip_group_check=True)
                if i % 2 == 1:
                    last = pe.matmul(o_bank[:, META:T], v_pair[:, i // 8, :], pT_meta[:, i // 2 % 2, :], start=False,
                                     stop=True, skip_group_check=True)
                last.then_inc(o_done, 1)

            def group(g, l):
                pe.wait_ge(mixed_ready, l * GROUPS + g + 1)
                if g == 0:
                    pe.wait_ge(w_grp_in, l * 16 + 16)
                    pe.wait_ge(r_ready, l * 3 + 2)
                else:
                    pe.wait_ge(zlo_ready, l * GROUPS + g)
                pe.matmul(small[:, S_BC:S_BC + T], w_grp[:, g, :], pool_u[:, g, PAD:], start=True, stop=True
                          ).then_inc(grp_done, 1)

            def after_kv(l, t0):
                for n in range(4):
                    unit(U_Q + n, l, T_Q + 2 * n, Q_BANKS[n], (8, 6, 4, 4)[n], KD, x_hi, x_lo, t0=t0)
                    if n == 2:
                        turn_v(l)
                unit(U_POOL, l, T_POOL, (2, 3), 2, KD, x_hi, x_lo)
                scores0(l)
                unit(U_POOL + 1, l, T_POOL + 2, (0, 1), 4, KD, x_hi, x_lo)
                for i in range(HEADS + 3):
                    if i < HEADS:
                        u, mt = U_GATE + i // 2, i % 2
                        if mt == 0:
                            unit_split(u, l)
                        tile_free(T_GATE + i, l, 2)
                        unit_tile(u, l, mt, mt, KD, x_hi, x_lo, t0)
                        scores(i, l)
                    if 2 <= i < HEADS + 2:
                        turn_p(i - 2, l)
                    if i >= 3:
                        attend(i - 3, l)
                    if i in GROUP_STEPS:
                        group(GROUP_STEPS.index(i), l)
                    if i >= HEADS:
                        m = i - HEADS
                        if m == 0:
                            pe.wait_ge(zlo_ready, (l + 1) * GROUPS)
                            pe.wait_ge(biased, (l + 1) * HEADS)
                        unit(U_PP + m, l, T_PP + 2 * m, (2 * (m % 2), 2 * (m % 2) + 1), 2 if m == 0 else 4,
                             GROUPS, z_hi, z_lo, t0=t0)
                unit(U_PP + 3, l, T_PP + 6, (2, 3), 4, GROUPS, z_hi, z_lo, t0=t0)
                pe.wait_ge(olo_ready, (l + 1) * KD)
                for m in range(4):
                    b = 2 * (m % 2)
                    unit(U_AP + m, l, T_AP + 2 * m, (b, b + 1), 4, KD, o_hi, o_lo, t0=t0)
                deep_pair(U_WO, l, x_hi, x_lo, lambda k: x_tile(2 * KD + k, l), t=T_WO, t0=t0)
                for m in range(2, 4):
                    b = 2 * (m % 2)
                    unit(U_WO + m, l, T_WO + 2 * m, (b, b + 1), 4, KD, x_hi, x_lo, t0=t0)
                sum_squares(3, l)
                keep_warm(WARM_RMS)
                spread_rms(3, l)
                keep_warm(WARM_X)
                ffn(1, l, t0)

            pe.wait_ge(inputs_in, 16 * 4)
            pe.wait_ge(consts, 1)
            pe.transpose(small[:, 0:n_rows], first_rows, ident[0:n_rows, 0:n_rows]).then_inc(first_T, 1)
            for k in range(KD):
                if k == KD // 2:
                    pe.wait_ge(second_half_in, 16)
                if k >= 4:
                    pe.wait_ge(h_ready, k - 3)
                b = bank[k % 4]
                pe.transpose(b[:, 0:META], first_meta[:, k * P:(k + 1) * P], ident[0:META, 0:META])
                pe.transpose(b[:, B1], first_x[:, 0, k * P:(k + 1) * P], ident[:, :])
                pe.transpose(b[:, B2], first_x[:, 1, k * P:(k + 1) * P], ident[:, :]).then_inc(first_T, 1)

            with pe.Fori(0, DEPTH) as l:
                ffn(0, l)
                deep_pair(U_K, l, x_hi, x_lo, lambda k: x_tile(KD + k, l), lambda: sum_squares(2, l))
                spread_rms(2, l)
                with pe.If(l < DEPTH - 1):
                    after_kv(l, 0)
                with pe.Else():
                    after_kv(l, META)

            for k in range(KD):
                pe.wait_ge((even_h_ready, odd_h_ready)[k % 2], k // 2 + 1)
                if k == 0:
                    pe.wait_ge(tile_read, DEPTH * TILES + TR0)
                for b in range(2):
                    last = pe.transpose(bank[2 * b + k // 4][:, k % 4 * P:(k % 4 + 1) * P], h[:, k, (B1, B2)[b]], ident[:, :])
                    if k % 4 == 3:
                        last.then_inc(final_T, 1)

        @block.scalar
        def _(act):
            act.sem_inc(silu_done, 2)

            def split_hi(u, l, more=0):
                act.wait_ge(raw_landed[u % RING], landed_at(u, l, more))
                act.wait_ge(unit_done, l * UNITS + u + 1 + (more * 4))
                for w, hi, _ in split_parts(u):
                    last = act.activation(hi, w, ACT.Copy)
                last.then_inc(hi_done, 1)

            def square(n, m, src, ready, at):
                act.wait_ge(ready, at)
                if m < 2:
                    act.wait_ge(ssq_done, n + 1)
                else:
                    act.wait_ge(acc_done, n * (KD - 3) + max(1, m - 2))
                act.activation(sq[:, m % 2, :], src, ACT.Square).then_inc(sq_done, 1)

            def last_square(n, last_bank, used):
                square(n, KD - 1, last_bank[:, 0:T], unit_done, used)

            def x_high(columns, h_before, k):
                act.wait_ge(h_ready, h_before + k + 1)
                act.activation(x_hi[:, k, :], h[:, k, :], ACT.Copy, scale=columns[:, k:k + 1]).then_inc(xhi_ready, 1)

            def pre_norm(n, columns, h_before):
                for k in range(KD):
                    x_high(columns, h_before, k)
                    square(n, k, h[:, k, :], h_ready, h_before + k + 1)

            def silus(f, l, pair, more=0):
                for j in range(2):
                    act.wait_ge(tile_read, l * TILES + T_FFN_IN[f] + 4 * pair + j + 1 + TR0 + more * 4)
                    act.wait_ge(hf_ready, l * 2 * KF + f * KF + 2 * pair + j + 1 + more * 2)
                    act.activation(silu[:, j, :], gate_r[:, j, :], ACT.Silu).then_inc(silu_done, 1)

            def ffn(f, l):
                u0 = U_FFN_IN[f]
                split_hi(u0 + 3, l)
                split_hi(u0 + 4, l)
                silus(f, l, 0)
                with act.Fori(0, 4) as i:
                    for j in range(4):
                        split_hi(u0 + 5 + j, l, i)
                        if j % 2 == 1:
                            silus(f, l, 1 + j // 2, i * 2)
                for j in range(18, 22):
                    split_hi(u0 + j + 3, l)
                    if j % 2 == 1:
                        silus(f, l, (j - 1) // 2)
                u0 = U_FFN_OUT[f]

                def out_squares(i):
                    for m in range(2 * i, min(2 * i + 2, KD - 1)):
                        square(l * NORMS + 4 * f + 1, m, y[:, m, :], tile_read,
                               l * TILES + T_FFN_OUT[f] + m + 1 + TR0)
                    if i == 3:
                        last_square(l * NORMS + 4 * f + 1, bank[3], l * UNITS + u0 + N_OUT + RING)

                for i in range(3):
                    for j in range(4):
                        split_hi(u0 + 3 + 4 * i + j, l)
                    out_squares(i)
                split_hi(u0 + 15, l)
                if f == 0:
                    split_hi(U_K, l)
                    split_hi(U_V, l)
                    split_hi(U_Q, l)
                    out_squares(3)
                else:
                    with act.If(l < DEPTH - 1):
                        split_hi(0, l + 1)
                        split_hi(1, l + 1)
                        split_hi(2, l + 1)
                    out_squares(3)

            def exps(i, l):
                act.wait_ge(neg_max, l * HEADS + i + 1)
                s, st = s_buf[:, i % 3, :], stats[:, i % 3, :]
                act.activation(s[:, 0:T], s[:, 0:T], ACT.Exp, bias=st[:, 2:3], accum_out=st[:, 4:5])
                act.activation(s[:, T:BAND], s[:, T:BAND], ACT.Exp, bias=st[:, 3:4], accum_out=st[:, 5:6])
                act.activation(st[:, 6:8], st[:, 2:4], ACT.Exp, bias=sink_cur[:, i:i + 1]).then_inc(exp_done, 1)

            def take_pT(i, l):
                act.wait_ge(pT_done, l * HEADS + i + 1)
                if i >= 2:
                    act.wait_ge(o_done, l * HEADS + i - 1)
                last = act.activation(pT[:, i % 2, :], pT_bank[:, 0:3 * P], ACT.Copy)
                if i % 2 == 1:
                    if i == 1:
                        act.wait_ge(consts, l + 2)
                    for b in range(2):
                        rows, cols = slice(2 * META * b, 2 * META * (b + 1)), slice(P * b, P * (b + 1))
                        last = act.activation(pT_meta[rows, i // 2 % 2, cols], pTm_bank[rows, 0:P], ACT.Copy)
                last.then_inc(pT_ready, 1)

            def tanh(m, l):
                act.wait_ge(tile_read, l * TILES + T_GATE + m + 1 + TR0)
                act.activation(gates[:, m, :], gates[:, m, :], ACT.Tanh, scale=0.5).then_inc(tanh_done, 1)

            def merge_hi(m, l):
                act.wait_ge(merged, l * KD + m + 1)
                act.activation(x_hi[:, m, :], gates[:, m, :], ACT.Copy, scale=0.5).then_inc(xhi_ready, 1)

            act.preload_act_table(ACT.Silu)
            act.wait_ge(layer_consts, 1)
            for u in range(2):
                for k in range(u * KD // 2, (u + 1) * KD // 2):
                    x_high(g_next, 0, k)
                split_hi(u, 0)
            act.dma_start(geo[:, :], geometry).then_inc(geo_in, 16)
            act.dma_start(sink_all[:, :], sinks.rearrange("(o l) h -> o (l h)", o=1).to_broadcast([P, DEPTH * HEADS])
                          ).then_inc(geo_in, 16)
            split_hi(2, 0)
            for k in range(KD):
                square(0, k, h[:, k, :], h_ready, k + 1)
            with act.Fori(0, DEPTH) as l:
                ffn(0, l)
                act.wait_ge(layer_consts, l + 2)
                pre_norm(l * NORMS + 2, g_cur[:, 2 * KD:3 * KD], l * 3 * KD + KD)
                act.preload_act_table(ACT.Exp)
                for u in range(41, 46):
                    split_hi(u, l)
                act.wait_ge(v_turned, l + 1)
                act.activation(v_tok[:, :, :], pT_bank[:, :].rearrange("p (b c) -> p b c", b=2), ACT.Copy
                               ).then_inc(v_ready, 1)
                act.activation(v_pair[:, :, :], pTm_bank[0:4 * META, KV_DIM:2 * KV_DIM].rearrange("p (j c) -> p j c", j=2),
                               ACT.Copy)
                act.activation(v_meta[:, :], pTm_bank[0:META, 0:KV_DIM], ACT.Copy).then_inc(v_ready, 1)
                for u in range(46, 49):
                    split_hi(u, l)
                for i in range(HEADS + 3):
                    if i == 0:
                        act.wait_ge(s0_step, l * S0_STEPS + S0_SHIFTED)
                        act.activation(s0[0:META, :, 0:META], s0[0:META, :, 0:META], ACT.Exp)
                        act.activation(stats0[:, 2, :], stats0[:, 1, :], ACT.Exp).then_inc(s0_exp, 1)
                    if 1 <= i <= HEADS:
                        tanh(i - 1, l)
                    if i % 2 == 0 and i < HEADS:
                        split_hi(49 + i // 2, l)
                    if i >= HEADS:
                        split_hi(57 + i - HEADS, l)
                    if 2 <= i < HEADS + 2:
                        take_pT(i - 2, l)
                    if i < HEADS:
                        exps(i, l)
                split_hi(60, l)
                for n in range(4):
                    split_hi(61 + n, l)
                    if n >= 1:
                        merge_hi(2 * n - 2, l)
                        merge_hi(2 * n - 1, l)
                merge_hi(6, l)
                merge_hi(7, l)
                act.preload_act_table(ACT.Silu)
                split_hi(65, l)
                split_hi(66, l)
                for m in range(4):
                    square(l * NORMS + 3, m, y[:, m, :], tile_read, l * TILES + T_WO + m + 1 + TR0)
                split_hi(67, l)
                for m in range(4, 6):
                    square(l * NORMS + 3, m, y[:, m, :], tile_read, l * TILES + T_WO + m + 1 + TR0)
                split_hi(68, l)
                square(l * NORMS + 3, 6, y[:, 6, :], tile_read, l * TILES + T_WO + 6 + 1 + TR0)
                last_square(l * NORMS + 3, bank[3], l * UNITS + U_WO + 4 + RING)
                pre_norm(l * NORMS + 4, g_cur[:, 4 * KD:5 * KD], l * 3 * KD + 2 * KD)
                ffn(1, l)
                with act.If(l < DEPTH - 1):
                    pre_norm(l * NORMS + NORMS, g_next, l * 3 * KD + 3 * KD)

            for n in range(3):
                act.wait_ge(final_T, n + 1)
                act.activation(out_sb[:, n % 2, n // 2 * (D // 2):(n // 2 + 1) * (D // 2)], bank[(0, 2, 1)[n]][:, :], ACT.Copy
                               ).then_inc(out_ready, 1)

        @block.vector
        def _(dve):
            dve.sem_inc(lo_done, RING)
            dve.sem_inc(tile_read, TR0)

            def split_lo(u, l, more=0):
                dve.wait_ge(hi_done, l * UNITS + u + 1 + more)
                for w, hi, lo in split_parts(u):
                    last = dve.tensor_tensor(lo, w, hi.bitcast(F32), ALU.subtract)
                last.then_inc(lo_done, 1)

            def split_lo_between(u, l, between):
                dve.wait_ge(hi_done, l * UNITS + u + 1)
                (w, hi, lo), (w2, hi2, lo2) = split_parts(u, halves=True)
                dve.tensor_tensor(lo, w, hi.bitcast(F32), ALU.subtract)
                between()
                dve.tensor_tensor(lo2, w2, hi2.bitcast(F32), ALU.subtract).then_inc(lo_done, 1)

            def tile_done(u, fin, l, mt, more_u=0, more_f=0):
                if mt == 0:
                    dve.wait_ge(first_done, l * FINISHERS + fin + 1 + more_f)
                else:
                    dve.wait_ge(unit_done, l * UNITS + u + RING + 1 + more_u)

            def layer_columns(l):
                dve.wait_ge(geo_in, 32)
                dve.wait_ge(xlo_ready, l * 4 * KD + KD)
                dve.wait_ge(h_ready, l * 3 * KD + KD)
                scales = DEPTH * NORMS * KD
                dve.tensor_copy(g_cur[:, :], g_all[:, ds(l * (NORMS * KD), NORMS * KD)])
                dve.tensor_copy(scale_cur[:, :], g_all[:, ds(l * GROUPS + scales, GROUPS)])
                for g in range(2):
                    dve.tensor_copy(sink_cur[:, 8 * g:8 * g + 8].rearrange("p (t s) -> p s t", s=2),
                                           sink_all[:, ds(l * HEADS + 8 * g, 8)].rearrange("p (s t) -> p s t", s=2))
                dve.tensor_scalar(half_g[:, :], g_all[:, ds(l * (NORMS * KD) + (NORMS - 1) * KD, KD)], 0.5, None, ALU.mult)
                dve.tensor_copy(g_next[:, :], g_all[:, ds(l * (NORMS * KD) + NORMS * KD, KD)]).then_inc(layer_consts, 1)
                dve.wait_ge(layer_consts, l + 2)

            def mean_square(q, l):
                dve.wait_ge(ssq_done, l * NORMS + q + 2)
                dve.tensor_scalar(var[:, 0:2], small[:, S_SUM:S_SUM + 2], 1.0 / D, EPS, ALU.mult, ALU.add)
                n = T - 2 * P
                dve.tensor_scalar(var[0:n, 2:3], small[0:n, S_SUM + 2:S_SUM + 3], 1.0 / D, EPS, ALU.mult, ALU.add
                                  ).then_inc(var_ready, 1)

            def take_rms(q, l):
                dve.wait_ge(bcast_done, l * NORMS + q + 1)
                dve.tensor_copy(r[:, :], small[:, S_BC:S_BC + T]).then_inc(r_ready, 1)
                dve.wait_ge(r_ready, l * 3 + q // 2 + 1)

            def x_low(at, columns, k):
                dve.wait_ge(xhi_ready, at + k + 1)
                dve.scalar_tensor_tensor(out=x_lo[:, k, :], in0=h[:, k, :], scalar=columns[:, k:k + 1],
                                         in1=x_hi[:, k, :].bitcast(F32), op0=ALU.mult, op1=ALU.subtract
                                         ).then_inc(xlo_ready, 1)

            def last_update(l):
                dve.wait_ge(bcast_done, l * NORMS + NORMS)
                for k in range(KD):
                    dve.scalar_tensor_tensor(out=y[:, k, META:T], in0=y[:, k, META:T], scalar=half_g[:, k:k + 1],
                                             in1=small[:, S_BC + META:S_BC + T], op0=ALU.mult, op1=ALU.mult
                                             ).then_inc(t_ready, 1)
                    if k % 2 == 1:
                        dve.wait_ge(t_ready, l * 3 * KD + 2 * KD + k + 1)
                        dve.tensor_tensor(h[:, k, META:T], h[:, k, META:T], y[:, k, META:T], ALU.add
                                          ).then_inc(odd_h_ready, 1)

            def boundary(n, l, at, columns):

                def normed(k):
                    dve.scalar_tensor_tensor(out=tmp[:, k % 2, 0:T], in0=y[:, k, :],
                                             scalar=g_cur[:, (2 * n + 1) * KD + k:(2 * n + 1) * KD + k + 1],
                                             in1=small[:, S_BC:S_BC + T], op0=ALU.mult, op1=ALU.mult
                                             ).then_inc(t_ready, 1)

                dve.wait_ge(bcast_done, l * NORMS + 2 * n + 2)
                normed(0)
                for k in range(KD):
                    dve.wait_ge(t_ready, l * 3 * KD + n * KD + k + 1)
                    dve.scalar_tensor_tensor(out=h[:, k, :], in0=tmp[:, k % 2, 0:T], scalar=1.0 if n == 1 else 0.5,
                                             in1=h[:, k, :], op0=ALU.mult, op1=ALU.add).then_inc(h_ready, 1)
                    if k >= 2:
                        x_low(at, columns, k - 1)
                    if k + 1 < KD:
                        normed(k + 1)
                    if k == 0:
                        x_low(at, columns, 0)
                x_low(at, columns, KD - 1)

            def take_gate(f, l, unit, mp=0):
                for j in range(2):
                    tile_done(U_FFN_IN[f] + unit, F_FFN_IN[f] + unit, l, j, mp * 2, mp * 2)
                    dve.wait_ge(silu_done, l * 2 * KF + f * KF + unit + j + 1 + mp * 2)
                    dve.tensor_tensor(gate_r[:, j, :], bank[4 * (unit // 2 % 2) + j][:, 0:T], r[:, :], ALU.mult).then_inc(tile_read, 1)

            def take_up(f, l, unit, mp=0):
                for j in range(2):
                    tile_done(U_FFN_IN[f] + unit, F_FFN_IN[f] + unit, l, j, mp * 2, mp * 2)
                    dve.wait_ge(hf_ready, l * 2 * KF + f * KF + unit - 1 + j + 1 + mp * 2)
                    dve.tensor_tensor(up_r[:, j, :], bank[2 + j][:, 0:T], r[:, :], ALU.mult).then_inc(tile_read, 1)

            def ffn(f, l):
                u0 = U_FFN_IN[f]
                split_lo_between(u0 + 3, l, lambda: mean_square(4 * f, l))
                take_rms(4 * f, l)
                take_gate(f, l, 0)
                split_lo(u0 + 4, l)
                with dve.Fori(0, 4) as i:
                    for j in range(4):
                        (take_up if j % 2 == 0 else take_gate)(f, l, 1 + j, i * 2)
                        split_lo(u0 + 5 + j, l, i * 4)
                for j in range(18, 22):
                    (take_up if j % 2 == 0 else take_gate)(f, l, j - 1, 0)
                    split_lo(u0 + j + 3, l)
                take_up(f, l, 21, 0)
                u0 = U_FFN_OUT[f]

                def take_out(i):
                    for j in range(2):
                        tile_done(u0 + 4 * i + 3, F_FFN_OUT[f] + i, l, j)
                        if (i, j) == (3, 1):
                            dve.wait_ge(sq_done, (l * NORMS + 4 * f + 2) * KD)
                        dve.tensor_copy(y[:, 2 * i + j, :], bank[2 * (i % 2) + j][:, 0:T]).then_inc(tile_read, 1)

                for i in range(3):
                    for j in range(4):
                        split_lo(u0 + 3 + 4 * i + j, l)
                    take_out(i)
                split_lo(u0 + 15, l)
                if f == 0:
                    split_lo(U_K, l)
                    split_lo(U_V, l)
                    take_out(3)
                    mean_square(1, l)
                    split_lo_between(U_Q, l, lambda: boundary(0, l, l * 4 * KD + KD, g_cur[:, 2 * KD:3 * KD]))
                else:
                    with dve.If(l < DEPTH - 1):
                        split_lo(0, l + 1)
                        split_lo(1, l + 1)
                    take_out(3)
                    mean_square(5, l)
                    with dve.If(l < DEPTH - 1):
                        split_lo_between(2, l + 1, lambda: boundary(2, l, l * 4 * KD + 4 * KD, g_next))
                    with dve.Else():
                        last_update(l)

            def take(u, fin, l, banks, how, last_square=None):
                for j in range(2):
                    tile_done(u, fin, l, j)
                    if j == 1 and last_square is not None:
                        dve.wait_ge(sq_done, last_square)
                    how(j, bank[banks[j]][:, 0:T]).then_inc(tile_read, 1)

            def spread_v(l):
                dve.wait_ge(tile_read, l * TILES + T_KV + 4 + TR0)
                dve.wait_ge(consts, l + 2)
                for side in range(2):
                    rows = slice(side * DH, (side + 1) * DH)
                    for b in range(2):
                        c = (2 * b + side) * META
                        last = dve.tensor_copy(vT_pair[rows, :, c:c + META], vT[rows, :, 0:META])
                last.then_inc(v_spread, 1)

            def take_q(n, l):
                take(U_Q + n, F_Q + n, l, Q_BANKS[n], lambda j, ps: dve.scalar_tensor_tensor(
                    out=qT[:, 2 * n + j, :], in0=ps, scalar=DH ** -0.5, in1=r[:, :], op0=ALU.mult, op1=ALU.mult))

            def take_pool(n, l):
                take(U_POOL + n, F_POOL + n, l, (2 - 2 * n, 3 - 2 * n), lambda j, ps: dve.tensor_tensor(
                    pool_u[:, 2 * n + j, PAD:], ps, r[:, :], ALU.mult))

            def take_gate_tile(m, l):
                tile_done(U_GATE + m // 2, F_GATE + m // 2, l, m % 2)
                dve.tensor_tensor(gates[:, m, :], bank[m % 2][:, 0:T], r[:, :], ALU.mult).then_inc(tile_read, 1)

            def step0(n, l, ins):
                ins.then_inc(s0_step, 1)
                dve.wait_ge(s0_step, l * S0_STEPS + n)

            p0 = s0[0:META, :, 0:META]

            def softmax0_shift(l):
                dve.wait_ge(s0_done, l + 1)
                dve.wait_ge(consts, l + 2)
                for side in range(2):
                    ps = (o_bank, small)[side][0:META, 0:HEADS // 2 * META].rearrange("p (c k) -> p c k", k=META)
                    last = dve.tensor_tensor(s0[0:META, side::2, 0:META], ps,
                                             causal0.unsqueeze(1).to_broadcast([META, HEADS // 2, META]), ALU.add)
                step0(1, l, last)
                step0(2, l, dve.reduce_max(stats0[:, 0, :], p0, AX_X))
                step0(3, l, dve.tensor_tensor(stats0[:, 0, :], stats0[:, 0, :], sink_cur[0:META, :], ALU.max))
                step0(4, l, dve.tensor_tensor(stats0[:, 1, :], sink_cur[0:META, :], stats0[:, 0, :], ALU.subtract))
                step0(5, l, dve.tensor_tensor(p0, p0, stats0[:, 0, :].unsqueeze(2).to_broadcast([META, HEADS, META]),
                                              ALU.subtract))

            def softmax0_sum(l):
                dve.wait_ge(s0_exp, l + 1)
                step0(6, l, dve.reduce_sum(stats0[:, 3, :], p0, AX_X))
                step0(7, l, dve.tensor_tensor(stats0[:, 3, :], stats0[:, 3, :], stats0[:, 2, :], ALU.add))

            def softmax0_scale(l):
                step0(8, l, dve.reciprocal(stats0[:, 3, :], stats0[:, 3, :]))
                step0(9, l, dve.tensor_tensor(p0, p0, stats0[:, 3, :].unsqueeze(2).to_broadcast([META, HEADS, META]),
                                              ALU.mult))
                step0(10, l, dve.transpose(p0T[:, :, :].rearrange("p h k -> p (h k)"),
                                           s0[:, :, :].rearrange("p h k -> p (h k)")))

            def bias_and_max(i, l):
                s, st = s_buf[:, i % 3, :], stats[:, i % 3, :]
                n = l * HEADS + i + 1
                dve.wait_ge(score_done, n)
                if i >= 3:
                    dve.wait_ge(pT_done, n - 3)
                dve.scalar_tensor_tensor(out=s, in0=distance, scalar=-slopes()[head_at(i)],
                                         in1=score_bank[i % 2][:, 0:BAND], op0=ALU.mult, op1=ALU.add
                                         ).then_inc(biased, 1)
                dve.wait_ge(biased, n)
                dve.reduce_max(st[:, 0:1], s[:, 0:T], AX_X)
                dve.reduce_max(st[:, 1:2], s[:, T:BAND], AX_X).then_inc(row_max, 1)
                dve.wait_ge(row_max, n)
                dve.tensor_scalar(st[:, 2:4], st[:, 0:2], sink_cur[:, i:i + 1], -1.0, ALU.max, ALU.mult
                                  ).then_inc(neg_max, 1)

            def invert_sum(i, l):
                st = stats[:, i % 3, :]
                n = l * HEADS + i + 1
                dve.wait_ge(exp_done, n)
                dve.tensor_tensor(st[:, 4:6], st[:, 4:6], st[:, 6:8], ALU.add).then_inc(den_ready, 1)
                dve.wait_ge(den_ready, n)
                dve.reciprocal(st[:, 0:2], st[:, 4:6]).then_inc(inv_ready, 1)

            def take_o(c, l):
                dve.wait_ge(o_done, l * HEADS + 2 * c + 2)
                dve.tensor_copy(o_hi[:, c, :], o_bank[:, 0:T]).then_inc(ohi_ready, 1)
                dve.wait_ge(ohi_ready, l * KD + c + 1)
                dve.tensor_tensor(o_lo[:, c, :], o_bank[:, 0:T], o_hi[:, c, :].bitcast(F32), ALU.subtract
                                  ).then_inc(olo_ready, 1)

            def mix(g, l):
                dve.wait_ge(win_done, l * GROUPS + g + 1)
                dve.scalar_tensor_tensor(out=pool_u[:, g, PAD:], in0=win[:, g % 2, PAD:],
                                         scalar=1.0 / POOL_WINDOWS[g], in1=pool_u[:, g, PAD:],
                                         op0=ALU.mult, op1=ALU.subtract).then_inc(mixed_ready, 1)

            def take_z(g, l):
                dve.wait_ge(grp_done, l * GROUPS + g + 1)
                ps = small[:, S_BC:S_BC + T]
                dve.tensor_scalar(z_hi[:, g, :], ps, scale_cur[:, g:g + 1], None, ALU.mult).then_inc(zhi_ready, 1)
                dve.wait_ge(zhi_ready, l * GROUPS + g + 1)
                dve.scalar_tensor_tensor(out=z_lo[:, g, :], in0=ps, scalar=scale_cur[:, g:g + 1],
                                         in1=z_hi[:, g, :].bitcast(F32), op0=ALU.mult, op1=ALU.subtract
                                         ).then_inc(zlo_ready, 1)

            def gated(first_gate, n, u, fin, l):
                b = 2 * (n % 2)
                dve.wait_ge(tanh_done, l * 2 * KD + first_gate + 2 * n + 2)

                def how(j, ps):
                    g = gates[:, first_gate + 2 * n + j, :]
                    return dve.scalar_tensor_tensor(out=g, in0=g, scalar=1.0, in1=ps, op0=ALU.add, op1=ALU.mult)

                take(u, fin, l, (b, b + 1), how)

            def merge_lo(m, l):
                dve.wait_ge(xhi_ready, l * 4 * KD + 2 * KD + m + 1)
                dve.scalar_tensor_tensor(out=x_lo[:, m, :], in0=gates[:, m, :], scalar=0.5,
                                         in1=x_hi[:, m, :].bitcast(F32), op0=ALU.mult, op1=ALU.subtract
                                         ).then_inc(xlo_ready, 1)

            dve.wait_ge(first_T, 1)
            dve.tensor_copy(g_all[:, :], small[:, 0:n_rows]).then_inc(rows_read, 1)
            for k in range(KD):
                dve.wait_ge(first_T, k + 2)
                dve.tensor_copy(h[:, k, :], bank[k % 4][:, 0:T]).then_inc(h_ready, 1)
                if k == KD // 2 - 1:
                    dve.wait_ge(rows_read, 1)
                    dve.tensor_copy(g_next[:, :], g_all[:, 0:KD]).then_inc(layer_consts, 1)
            dve.wait_ge(layer_consts, 1)
            for u in range(2):
                for k in range(u * KD // 2, (u + 1) * KD // 2):
                    x_low(0, g_next, k)
                split_lo(u, 0)
            split_lo(2, 0)

            with dve.Fori(0, DEPTH) as l:
                layer_columns(l)
                ffn(0, l)
                mean_square(2, l)
                split_lo(41, l)
                take_rms(2, l)
                take(U_K, F_KV, l, (0, 1), lambda j, ps: dve.tensor_tensor(kT[:, j, :], ps, r[:, :], ALU.mult))
                take(U_V, F_KV + 1, l, (2, 3), lambda j, ps: dve.tensor_tensor(vT[:, j, :], ps, r[:, :], ALU.mult))
                split_lo(42, l)
                split_lo(43, l)
                spread_v(l)
                for n in range(4):
                    take_q(n, l)
                    split_lo(44 + n, l)
                take_pool(0, l)
                softmax0_shift(l)
                split_lo(48, l)
                take_pool(1, l)
                for i in range(HEADS + 1):
                    if 5 <= i < HEADS and i % 2 == 1:
                        take_o((i - 5) // 2, l)
                    if 1 <= i <= HEADS:
                        take_gate_tile(i - 1, l)
                        invert_sum(i - 1, l)
                    if i - 1 in GROUP_STEPS:
                        take_z(GROUP_STEPS.index(i - 1), l)
                    if i % 2 == 1 and i < HEADS:
                        split_lo(49 + i // 2, l)
                    if i < HEADS:
                        bias_and_max(i, l)
                    if i == 0:
                        softmax0_sum(l)
                    if i == 2:
                        softmax0_scale(l)
                    if i in MIX_STEPS:
                        mix(MIX_STEPS.index(i), l)
                take_o(6, l)
                split_lo(57, l)
                split_lo(58, l)
                gated(0, 0, U_PP, F_PP, l)
                gated(0, 1, U_PP + 1, F_PP + 1, l)
                take_o(7, l)
                gated(0, 2, U_PP + 2, F_PP + 2, l)
                split_lo(59, l)
                gated(0, 3, U_PP + 3, F_PP + 3, l)
                split_lo(60, l)
                for n in range(4):
                    split_lo(61 + n, l)
                    gated(KD, n, U_AP + n, F_AP + n, l)
                    if n >= 1:
                        merge_lo(2 * n - 2, l)
                        merge_lo(2 * n - 1, l)
                merge_lo(6, l)
                merge_lo(7, l)
                split_lo(65, l)

                def take_y(n):
                    b = 2 * (n % 2)
                    take(U_WO + n, F_WO + n, l, (b, b + 1), lambda j, ps: dve.tensor_copy(y[:, 2 * n + j, :], ps),
                         (l * NORMS + 4) * KD if n == 3 else None)

                take_y(0)
                take_y(1)
                split_lo(66, l)
                split_lo(67, l)
                take_y(2)
                take_y(3)
                mean_square(3, l)
                split_lo_between(68, l, lambda: boundary(1, l, l * 4 * KD + 3 * KD, g_cur[:, 4 * KD:5 * KD]))
                ffn(1, l)

            dve.wait_ge(final_T, 4)
            dve.tensor_copy(out_sb[:, 1, D // 2:D], bank[3][:, :]).then_inc(out_late, 1)

        @block.gpsimd
        def _(pool):
            pool.sem_inc(hf_ready, 2)
            pool.memset(ident[:, :], 0.0).then_inc(win_step, 1)
            pool.memset(half[:, :], -0.5)
            pool.memset(var[:, :], 1.0)
            pool.memset(ones[:, :], 1.0)
            pool.wait_ge(win_step, 1)
            pool.affine_select(out=ident[:, :], in_=ident[:, :], compare_op=ALU.not_equal, fill=1.0, base=0,
                               pattern=[[-1, P]], channel_multiplier=1).then_inc(consts, 1)

            def add_squares(q, l):
                for m in range(1, KD - 2):
                    pool.wait_ge(sq_done, (l * NORMS + q) * KD + m + 1)
                    if m == 1:
                        pool.wait_ge(ssq_done, l * NORMS + q + 1)
                        pool.tensor_tensor(acc[:, :], sq[:, 0, :], sq[:, 1, :], ALU.add).then_inc(acc_done, 1)
                    else:
                        pool.wait_ge(acc_done, (l * NORMS + q) * (KD - 3) + m - 1)
                        pool.tensor_tensor(acc[:, :], acc[:, :], sq[:, m % 2, :], ALU.add).then_inc(acc_done, 1)

            def inverse_rms(q, l):
                pool.wait_ge(var_ready, l * NORMS + q + 1)
                pool.tensor_tensor(rt[:, 0:3], var[:, 0:3], half[:, 0:3], ALU.pow).then_inc(rt_ready, 1)

            def ffn(f, l):
                add_squares(4 * f, l)
                inverse_rms(4 * f, l)
                with pool.Fori(0, KF // 2) as i:
                    for j in range(2):
                        n = l * 2 * KF + f * KF + i * 2 + j
                        pool.wait_ge(silu_done, n + 3)
                        pool.wait_ge(tile_read, l * TILES + T_FFN_IN[f] + i * 4 + 3 + j + TR0)
                        pool.tensor_tensor(hid_hi[:, ds(i * 2 + j, 1), :].rearrange("p o t -> p (o t)"), silu[:, j, :],
                                           up_r[:, j, :], ALU.mult).then_inc(hid_hi_ready, 1)
                        pool.tensor_tensor(hid_f[:, j, :], silu[:, j, :], up_r[:, j, :], ALU.mult).then_inc(hf_ready, 1)
                        pool.wait_ge(hid_hi_ready, n + 1)
                        pool.wait_ge(hf_ready, n + 3)
                        pool.tensor_tensor(hid_lo[:, ds(i * 2 + j, 1), :].rearrange("p o t -> p (o t)"), hid_f[:, j, :],
                                           hid_hi[:, ds(i * 2 + j, 1), :].rearrange("p o t -> p (o t)").bitcast(F32),
                                           ALU.subtract).then_inc(hid_ready, 1)
                add_squares(4 * f + 1, l)
                inverse_rms(4 * f + 1, l)

            def window(g, l):
                done = sum(n + 2 for n in range(g))
                src, at = pool_u[:, g, :], 0
                for d in range(g + 1):
                    lag = 1 << d
                    dst = win[:, (2 * g - d) % 2, :]
                    a = at + lag
                    pool.tensor_tensor(dst[:, a:], src[:, a:], src[:, a - lag:PAD + T - lag], ALU.add
                                       ).then_inc(win_step, 1)
                    src, at = dst, a
                    pool.wait_ge(win_step, l * WIN_STEPS + done + d + 2)
                pool.tensor_tensor(src[:, PAD:2 * PAD], src[:, PAD:2 * PAD], ramp[:, g, :], ALU.mult
                                   ).then_inc(win_step, 1)
                pool.wait_ge(win_step, l * WIN_STEPS + done + g + 3)
                pool.sem_inc(win_done, 1)

            def normalise(i, l):
                s, st = s_buf[:, i % 3, :], stats[:, i % 3, :]
                pool.wait_ge(inv_ready, l * HEADS + i + 1)
                for b, keys in ((1, s[:, 0:T]), (0, s[:, T:BAND])):
                    inv = st[:, 1 - b:2 - b]
                    n, c = keys.shape[1] - META, i // 2 % 2 * P + (2 * b + i % 2) * META
                    pool.tensor_tensor(p_meta[:, c:c + META], keys[:, 0:META], inv.to_broadcast([P, META]), ALU.mult)
                    last = pool.tensor_tensor(keys[:, META:], keys[:, META:], inv.to_broadcast([P, n]), ALU.mult)
                last.then_inc(p_ready, 1)

            with pool.Fori(0, DEPTH) as l:
                ffn(0, l)
                add_squares(2, l)
                inverse_rms(2, l)
                pool.memset(pool_u[:, :, 0:PAD], 0.0)
                pool.memset(vT_pair, 0.0)
                pool.memset(pT_meta[:, :, :], 0.0)
                pool.memset(s0[:, :, :], 0.0).then_inc(consts, 1)
                pool.wait_ge(consts, l + 2)
                for i in range(HEADS + 1):
                    if i in WINDOW_STEPS:
                        g = WINDOW_STEPS.index(i)
                        pool.wait_ge(tile_read, l * TILES + T_POOL + g + 1 + TR0)
                        if g >= 1:
                            pool.wait_ge(mixed_ready, l * GROUPS + g)
                        window(g, l)
                    if i >= 1:
                        normalise(i - 1, l)
                for m in range(KD):
                    pool.wait_ge(tile_read, l * TILES + T_AP + m + 1 + TR0)
                    pool.tensor_tensor(gates[:, m, :], gates[:, m, :], gates[:, KD + m, :], ALU.add
                                       ).then_inc(merged, 1)
                add_squares(3, l)
                inverse_rms(3, l)
                ffn(1, l)

            for k in range(0, KD, 2):
                pool.wait_ge(t_ready, DEPTH * 3 * KD - KD + k + 1)
                pool.tensor_tensor(h[:, k, META:T], h[:, k, META:T], y[:, k, META:T], ALU.add).then_inc(even_h_ready, 1)


Q_BANKS = ((4, 5), (0, 1), (2, 3), (0, 1))
WARM_RMS, WARM_X = 5, 8
WINDOW_STEPS = (0, 2, 4, 6)
MIX_STEPS = (1, 3, 5, 7)
GROUP_STEPS = (3, 5, 7, 9)
S0_STEPS, S0_SHIFTED = 10, 5


def geometry_table():
    keys = np.arange(T)
    parts = []
    for first, n_keys in ((META + P, T), (META, META + P)):
        d = (first + np.arange(P))[:, None] - keys[None, :n_keys]
        parts.append(np.where(keys[None, :n_keys] < META, 0.0, np.where((d >= 0) & (d < WINDOW), d, FAR)))
    k = np.arange(META)
    mask = np.where(k[None, :] <= (np.arange(P)[:, None] % META), 0.0, -1e30)
    parts.append(mask)
    t = np.arange(PAD) + 1
    parts.append(np.tile(np.concatenate([w / np.minimum(t, w) for w in POOL_WINDOWS])[None], (P, 1)))
    return np.concatenate(parts, axis=1).astype(np.float32)


_INS = ["x", "meta_tokens", "norm_g", "ffn_w_in", "ffn_w_out", "w_in", "pool_w_grp", "pool_scale",
        "w_pool_proj", "sinks", "w_attn_proj", "w_o"]


def kernel(**inputs):
    import concourse.bacc as bacc
    from concourse.bass_utils import run_bass_kernel_spmd

    nc = bacc.Bacc("TRN2", target_bir_lowering=False, num_devices=1)
    arrays, args = {}, []
    for name in _INS + ["geometry"]:
        a = geometry_table() if name == "geometry" else np.ascontiguousarray(inputs[name])
        arrays[f"in_{name}"] = a
        args.append(nc.dram_tensor(f"in_{name}", a.shape, F32, kind="ExternalInput").ap())
    args.append(nc.dram_tensor("out_h", (1, SEQ, D), F32, kind="ExternalOutput").ap())
    trunk(nc, *args)
    result = run_bass_kernel_spmd(nc, [arrays], core_ids=[0])
    return result.results[0]["out_h"]
```
